# Optimizing a Trainium2 kernel written in Bass

```python
import math
import jax, jax.numpy as jnp
from jax import lax
import numpy as np
import jax
import jax.numpy as jnp

D_MODEL = 1024
BATCH = 1
SEQ = 256
DEPTH = 1

CHUNK = 64
N_MEM = 256
SB_HEADS = 8
SB_HEAD_DIM = 64
SB_WIDTH = SB_HEADS * SB_HEAD_DIM
SB_BLOCK = 128
CONV_CH = 256
CONV_WIDTH = 31
SSM_CH = 256
SSM_GROUP = 16
SSM_GROUPS = SSM_CH // SSM_GROUP
SSM_STATE = 64
MIX_WIDTH = SB_WIDTH + CONV_CH + SSM_CH
IN_PROJ = 3 * SB_WIDTH + 2 * CONV_CH + SSM_CH
XA_HEADS = 4
XA_HEAD_DIM = D_MODEL // XA_HEADS
XA_WIDTH = XA_HEADS * XA_HEAD_DIM
FFN_HIDDEN = ((int(math.ceil(8 * D_MODEL / 3)) + 255) // 256) * 256
EPS = 1e-6


def rms_norm(x, g):
    xf = x.astype(jnp.float32)
    y = xf * lax.rsqrt(jnp.mean(xf * xf, axis=-1, keepdims=True) + EPS)
    return (y * g.astype(jnp.float32)).astype(x.dtype)

def layer_norm(x, g, b):
    xf = x.astype(jnp.float32)
    mu = jnp.mean(xf, axis=-1, keepdims=True)
    var = jnp.mean(jnp.square(xf - mu), axis=-1, keepdims=True)
    y = (xf - mu) * lax.rsqrt(var + EPS)
    return (y * g.astype(jnp.float32) + b.astype(jnp.float32)).astype(x.dtype)

def stick_breaking_attention(q, k, v):
    bsz, L, H, hd = q.shape
    nb = L // SB_BLOCK
    kh = k.transpose(0, 2, 1, 3)
    vh = v.transpose(0, 2, 1, 3)
    q_blocks = q.transpose(0, 2, 1, 3).reshape(bsz, H, nb, SB_BLOCK, hd).transpose(2, 0, 1, 3, 4)
    key_pos = jnp.arange(L)
    scale = hd ** -0.5

    def one_block(args):
        qb, blk = args
        z = jnp.einsum('bhqd,bhkd->bhqk', qb, kh).astype(jnp.float32) * scale
        q_pos = blk * SB_BLOCK + jnp.arange(SB_BLOCK)
        mask = key_pos[None, :] < q_pos[:, None]
        log_1mb = jnp.where(mask, jax.nn.log_sigmoid(-z), 0.0)
        later = lax.cumsum(log_1mb, axis=3, reverse=True) - log_1mb
        w = jnp.where(mask, jnp.exp(jax.nn.log_sigmoid(z) + later), 0.0)
        return jnp.einsum('bhqk,bhkd->bhqd', w.astype(vh.dtype), vh)

    out = lax.map(one_block, (q_blocks, jnp.arange(nb)))
    return out.transpose(1, 0, 3, 2, 4).reshape(bsz, L, H * hd)

def conformer_conv(u2, dw_w, dw_b, ln_g, ln_b, pw2_w):
    a, b = jnp.split(u2, 2, axis=-1)
    h = a * jax.nn.sigmoid(b)
    h = lax.conv_general_dilated(
        h, dw_w[:, None, :].astype(h.dtype), window_strides=(1,),
        padding=((CONV_WIDTH - 1, 0),), dimension_numbers=('NWC', 'WIO', 'NWC'),
        feature_group_count=CONV_CH) + dw_b
    h = jax.nn.silu(layer_norm(h, ln_g, ln_b))
    return h @ pw2_w

def s5_ssm(u, lam_re, lam_im, log_dt, b_re, b_im, c_re, c_im, d, glu_w):
    bsz, L, _ = u.shape
    f32 = jnp.float32
    uf = u.astype(f32).reshape(bsz, L, SSM_GROUPS, SSM_GROUP)
    lr, li = lam_re.astype(f32), lam_im.astype(f32)
    dt = jnp.exp(log_dt.astype(f32))[:, None]
    mag = jnp.exp(lr * dt)
    ar, ai = mag * jnp.cos(li * dt), mag * jnp.sin(li * dt)
    den = lr * lr + li * li
    fr = ((ar - 1.0) * lr + ai * li) / den
    fi = (ai * lr - (ar - 1.0) * li) / den
    br, bi = b_re.astype(f32), b_im.astype(f32)
    bbr = fr[..., None] * br - fi[..., None] * bi
    bbi = fr[..., None] * bi + fi[..., None] * br
    bu_r = jnp.einsum('blgh,gph->blgp', uf, bbr)
    bu_i = jnp.einsum('blgh,gph->blgp', uf, bbi)
    shape = bu_r.shape
    a_r = jnp.broadcast_to(ar, shape)
    a_i = jnp.broadcast_to(ai, shape)

    def combine(e1, e2):
        a1r, a1i, b1r, b1i = e1
        a2r, a2i, b2r, b2i = e2
        return (a2r * a1r - a2i * a1i,
                a2r * a1i + a2i * a1r,
                a2r * b1r - a2i * b1i + b2r,
                a2r * b1i + a2i * b1r + b2i)

    _, _, xr, xi = lax.associative_scan(combine, (a_r, a_i, bu_r, bu_i), axis=1)
    y = (jnp.einsum('blgp,ghp->blgh', xr, c_re.astype(f32))
         - jnp.einsum('blgp,ghp->blgh', xi, c_im.astype(f32)))
    y = y.reshape(bsz, L, SSM_CH) + d.astype(f32) * uf.reshape(bsz, L, SSM_CH)
    y = y.astype(u.dtype)
    ya, yb = jnp.split(y @ glu_w, 2, axis=-1)
    return ya * jax.nn.sigmoid(yb)

def memory_cross_attention(h, m, wq, wk, wv, q_g, k_g, wo):
    bsz, L, _ = h.shape
    q = rms_norm((h @ wq).reshape(bsz, L, XA_HEADS, XA_HEAD_DIM), q_g)
    k = rms_norm((m @ wk).reshape(bsz, N_MEM, XA_HEADS, XA_HEAD_DIM), k_g)
    v = (m @ wv).reshape(bsz, N_MEM, XA_HEADS, XA_HEAD_DIM)
    s = jnp.einsum('blhd,bmhd->bhlm', q, k).astype(jnp.float32) * (XA_HEAD_DIM ** -0.5)
    p = jax.nn.softmax(s, axis=-1).astype(v.dtype)
    o = jnp.einsum('bhlm,bmhd->blhd', p, v).reshape(bsz, L, XA_WIDTH)
    return o @ wo

def first_inputs(seed: int = 0) -> dict:
    key = jax.random.key(seed)
    ks = iter(jax.random.split(key, 40))
    f32 = jnp.float32

    def nrm(shape, scale):
        return jax.random.normal(next(ks), shape, f32) * scale

    def gain(shape):
        return 1.0 + 0.02 * jax.random.normal(next(ks), shape, f32)

    n_idx = jnp.arange(SSM_STATE, dtype=f32)
    return {
        "x": nrm((BATCH, SEQ, D_MODEL), 1.0),
        "mem": nrm((BATCH, N_MEM, D_MODEL), 1.0),
        "norm_mix_g": gain((DEPTH, D_MODEL)),
        "w_in": nrm((DEPTH, D_MODEL, IN_PROJ), D_MODEL ** -0.5),
        "sb_q_norm_g": gain((DEPTH, SB_HEAD_DIM)),
        "sb_k_norm_g": gain((DEPTH, SB_HEAD_DIM)),
        "conv_dw_w": nrm((DEPTH, CONV_WIDTH, CONV_CH), CONV_WIDTH ** -0.5),
        "conv_dw_b": nrm((DEPTH, CONV_CH), 0.02),
        "conv_ln_g": gain((DEPTH, CONV_CH)),
        "conv_ln_b": nrm((DEPTH, CONV_CH), 0.02),
        "conv_pw2_w": nrm((DEPTH, CONV_CH, CONV_CH), CONV_CH ** -0.5),
        "ssm_lam_re": -0.5 * jnp.exp(nrm((DEPTH, SSM_GROUPS, SSM_STATE), 0.05)),
        "ssm_lam_im": jnp.pi * n_idx * jnp.exp(nrm((DEPTH, SSM_GROUPS, SSM_STATE), 0.01)),
        "ssm_log_dt": jax.random.uniform(next(ks), (DEPTH, SSM_GROUPS), f32,
                                         math.log(1e-3), math.log(1e-1)),
        "ssm_b_re": nrm((DEPTH, SSM_GROUPS, SSM_STATE, SSM_GROUP), (2 * SSM_GROUP) ** -0.5),
        "ssm_b_im": nrm((DEPTH, SSM_GROUPS, SSM_STATE, SSM_GROUP), (2 * SSM_GROUP) ** -0.5),
        "ssm_c_re": nrm((DEPTH, SSM_GROUPS, SSM_GROUP, SSM_STATE), (2 * SSM_STATE) ** -0.5),
        "ssm_c_im": nrm((DEPTH, SSM_GROUPS, SSM_GROUP, SSM_STATE), (2 * SSM_STATE) ** -0.5),
        "ssm_d": nrm((DEPTH, SSM_CH), 1.0),
        "ssm_glu_w": nrm((DEPTH, SSM_CH, 2 * SSM_CH), SSM_CH ** -0.5),
        "branch_norm_g": gain((DEPTH, MIX_WIDTH)),
        "w_out": nrm((DEPTH, MIX_WIDTH, D_MODEL), MIX_WIDTH ** -0.5),
        "norm_xa_g": gain((DEPTH, D_MODEL)),
        "norm_mem_g": gain((DEPTH, D_MODEL)),
        "xa_wq": nrm((DEPTH, D_MODEL, XA_WIDTH), D_MODEL ** -0.5),
        "xa_wk": nrm((DEPTH, D_MODEL, XA_WIDTH), D_MODEL ** -0.5),
        "xa_wv": nrm((DEPTH, D_MODEL, XA_WIDTH), D_MODEL ** -0.5),
        "xa_q_norm_g": gain((DEPTH, XA_HEAD_DIM)),
        "xa_k_norm_g": gain((DEPTH, XA_HEAD_DIM)),
        "xa_wo": nrm((DEPTH, XA_WIDTH, D_MODEL), XA_WIDTH ** -0.5),
        "norm_ffn_g": gain((DEPTH, D_MODEL)),
        "ffn_w_in": nrm((DEPTH, D_MODEL, 2 * FFN_HIDDEN), D_MODEL ** -0.5),
        "ffn_w_out": nrm((DEPTH, FFN_HIDDEN, D_MODEL), FFN_HIDDEN ** -0.5),
    }

def first_block(x, mem, norm_mix_g, w_in, sb_q_norm_g, sb_k_norm_g, conv_dw_w, conv_dw_b,
              conv_ln_g, conv_ln_b, conv_pw2_w, ssm_lam_re, ssm_lam_im, ssm_log_dt,
              ssm_b_re, ssm_b_im, ssm_c_re, ssm_c_im, ssm_d, ssm_glu_w, branch_norm_g,
              w_out, norm_xa_g, norm_mem_g, xa_wq, xa_wk, xa_wv, xa_q_norm_g, xa_k_norm_g,
              xa_wo, norm_ffn_g, ffn_w_in, ffn_w_out):
    bsz, L, _ = x.shape
    s1 = SB_WIDTH
    s2 = 2 * SB_WIDTH
    s3 = 3 * SB_WIDTH
    s4 = s3 + 2 * CONV_CH
    for l in range(DEPTH):
        h = rms_norm(x, norm_mix_g[l])
        p = h @ w_in[l]
        q = rms_norm(p[..., :s1].reshape(bsz, L, SB_HEADS, SB_HEAD_DIM), sb_q_norm_g[l])
        k = rms_norm(p[..., s1:s2].reshape(bsz, L, SB_HEADS, SB_HEAD_DIM), sb_k_norm_g[l])
        v = p[..., s2:s3].reshape(bsz, L, SB_HEADS, SB_HEAD_DIM)
        o_sb = stick_breaking_attention(q, k, v)
        o_conv = conformer_conv(p[..., s3:s4], conv_dw_w[l], conv_dw_b[l],
                                conv_ln_g[l], conv_ln_b[l], conv_pw2_w[l])
        o_ssm = s5_ssm(p[..., s4:], ssm_lam_re[l], ssm_lam_im[l], ssm_log_dt[l],
                       ssm_b_re[l], ssm_b_im[l], ssm_c_re[l], ssm_c_im[l],
                       ssm_d[l], ssm_glu_w[l])
        g = branch_norm_g[l]
        mixed = jnp.concatenate([
            rms_norm(o_sb, g[:SB_WIDTH]),
            rms_norm(o_conv, g[SB_WIDTH:SB_WIDTH + CONV_CH]),
            rms_norm(o_ssm, g[SB_WIDTH + CONV_CH:]),
        ], axis=-1)
        x = x + mixed @ w_out[l]
        hx = rms_norm(x, norm_xa_g[l])
        hm = rms_norm(mem, norm_mem_g[l])
        x = x + memory_cross_attention(hx, hm, xa_wq[l], xa_wk[l], xa_wv[l],
                                       xa_q_norm_g[l], xa_k_norm_g[l], xa_wo[l])
        hf = rms_norm(x, norm_ffn_g[l])
        gate, up = jnp.split(hf @ ffn_w_in[l], 2, axis=-1)
        x = x + (jax.nn.silu(gate) * up) @ ffn_w_out[l]
    return x


CTX_LEN = 256
GRID_W = 64

ML_WIDTH = D_MODEL // 2
ML_HEADS = 4
ML_HEAD_DIM = ML_WIDTH // ML_HEADS
ML_CHUNK = 128
GLA_WIDTH = D_MODEL - ML_WIDTH
GLA_HEADS = 4
GLA_DV = GLA_WIDTH // GLA_HEADS
GLA_KEY_WIDTH = GLA_WIDTH // 2
GLA_DK = GLA_KEY_WIDTH // GLA_HEADS
GLA_RANK = 16
GLA_TAU = 16.0
GLA_CHUNK = 64
CONV_W = 3
MIX_WIDTH_2 = ML_WIDTH + GLA_WIDTH
PROJ_WIDTHS = (ML_WIDTH, ML_WIDTH, ML_WIDTH, ML_WIDTH, 4 * ML_HEADS,
               GLA_KEY_WIDTH, GLA_KEY_WIDTH, GLA_WIDTH, GLA_WIDTH, 2 * GLA_RANK)
P_TOTAL = sum(PROJ_WIDTHS)

PEER_HEADS = 8
PEER_NKEYS = 128
PEER_EXPERTS = PEER_NKEYS * PEER_NKEYS
PEER_TOPK = 16
PEER_QDIM = 256
PEER_BLOCK = 128


def rms_norm_2(x, g):
    xf = x.astype(jnp.float32)
    y = xf * lax.rsqrt(jnp.mean(xf * xf, axis=-1, keepdims=True) + EPS)
    return y.astype(x.dtype) * g

def head_rms(h, g):
    y = h * lax.rsqrt(jnp.mean(h * h, axis=-1, keepdims=True) + EPS)
    return y.reshape(h.shape[:2] + (-1,)) * g

def short_conv(u, w, on_grid):
    bz, n, ch = u.shape
    if on_grid:
        rows = n // GRID_W
        u = u.reshape(bz * rows, GRID_W, ch)
    y = lax.conv_general_dilated(u, w[:, None, :].astype(u.dtype), (1,),
                                 [(CONV_W // 2, CONV_W // 2)],
                                 dimension_numbers=('NWC', 'WIO', 'NWC'),
                                 feature_group_count=ch)
    return y.reshape(bz, n, ch)

def to_chunks(t, size):
    bz, n, hh = t.shape[:3]
    t = t.reshape((bz, n // size, size, hh) + t.shape[3:])
    return jnp.moveaxis(t, 3, 1)

def from_chunks(t):
    bz, hh, nc, ll, d = t.shape
    return jnp.moveaxis(t, 1, 3).reshape(bz, nc * ll, hh, d)

def orient(t, direction):
    return jnp.flip(t, axis=1) if direction == 1 else t

def prep_mixers(z, conv_w, gate_b, lr_w2, alpha_b, on_grid):
    bz, n, _ = z.shape
    f32 = jnp.float32
    mq, mk, mv, mo, mg, gq, gk, gv, gr, glr = jnp.split(
        z, np.cumsum(PROJ_WIDTHS)[:-1].tolist(), axis=-1)
    mq, mk = jnp.split(jax.nn.silu(short_conv(jnp.concatenate([mq, mk], axis=-1), conv_w, on_grid)),
                       2, axis=-1)
    gates = (mg + gate_b).astype(f32).reshape(bz, n, 2, 2, ML_HEADS)
    alpha = jnp.einsum('bndr,drk->bndk', glr.reshape(bz, n, 2, GLA_RANK), lr_w2) + alpha_b
    return {
        'ml_q': mq.astype(f32).reshape(bz, n, ML_HEADS, ML_HEAD_DIM),
        'ml_k': (mk.astype(f32) * ML_HEAD_DIM ** -0.5).reshape(bz, n, ML_HEADS, ML_HEAD_DIM),
        'ml_v': mv.astype(f32).reshape(bz, n, ML_HEADS, ML_HEAD_DIM),
        'ml_o': mo,
        'ml_ig': gates[:, :, :, 0],
        'ml_lf': jax.nn.log_sigmoid(gates[:, :, :, 1]),
        'gla_q': (gq.astype(f32) * GLA_DK ** -0.5).reshape(bz, n, GLA_HEADS, GLA_DK),
        'gla_k': gk.astype(f32).reshape(bz, n, GLA_HEADS, GLA_DK),
        'gla_v': gv.astype(f32).reshape(bz, n, GLA_HEADS, GLA_DV),
        'gla_r': gr,
        'gla_la': (jax.nn.log_sigmoid(alpha.astype(f32)) / GLA_TAU).reshape(
            bz, n, 2, GLA_HEADS, GLA_DK),
    }

def mlstm_states(k, v, logf, ig, init):
    b = jnp.cumsum(logf, axis=-1)
    b_end = b[..., -1]
    w_log = b_end[..., None] - b + ig
    m_loc = jnp.max(w_log, axis=-1)
    w = jnp.exp(w_log - m_loc[..., None])
    c_loc = jnp.einsum('bhcld,bhcle->bhcde', w[..., None] * v, k)
    n_loc = jnp.einsum('bhcl,bhcle->bhce', w, k)

    def step(carry, inp):
        cm, nv, m = carry
        be, ml, cl, nl = inp
        m_new = jnp.maximum(be + m, ml)
        a = jnp.exp(be + m - m_new)
        bb = jnp.exp(ml - m_new)
        c_new = a[..., None, None] * cm + bb[..., None, None] * cl
        n_new = a[..., None] * nv + bb[..., None] * nl
        return (c_new, n_new, m_new), (cm, nv, m)

    xs = tuple(jnp.moveaxis(t, 2, 0) for t in (b_end, m_loc, c_loc, n_loc))
    final, starts = lax.scan(step, init, xs)
    starts = tuple(jnp.moveaxis(t, 0, 2) for t in starts)
    return starts, final

def mlstm_outputs(q, k, v, logf, ig, starts):
    c_s, n_s, m_s = starts
    ll = q.shape[-2]
    tri = jnp.tril(jnp.ones((ll, ll), dtype=bool))
    b = jnp.cumsum(logf, axis=-1)
    d_log = jnp.where(tri, b[..., :, None] - b[..., None, :] + ig[..., None, :], -jnp.inf)
    inter_log = b + m_s[..., None]
    m_t = jnp.maximum(inter_log, jnp.max(d_log, axis=-1))
    scores = jnp.einsum('bhctd,bhcsd->bhcts', q, k) * jnp.exp(d_log - m_t[..., None])
    inter = jnp.exp(inter_log - m_t)
    num = (jnp.einsum('bhcts,bhcsd->bhctd', scores, v)
           + inter[..., None] * jnp.einsum('bhcde,bhcte->bhctd', c_s, q))
    den = scores.sum(-1) + inter * jnp.einsum('bhce,bhcte->bhct', n_s, q)
    return num / jnp.maximum(jnp.abs(den), jnp.exp(-m_t))[..., None]

def mlstm_direction(lat, ctx, with_ctx_out):
    q, k, v, lf, ig = lat
    qc, kc, vc, lfc, igc = ctx
    bz, hh, _, _, d = q.shape
    init = (jnp.zeros((bz, hh, d, d), jnp.float32), jnp.zeros((bz, hh, d), jnp.float32),
            jnp.zeros((bz, hh), jnp.float32))
    ctx_starts, ctx_final = mlstm_states(kc, vc, lfc, igc, init)
    lat_starts, _ = mlstm_states(k, v, lf, ig, ctx_final)
    h = mlstm_outputs(q, k, v, lf, ig, lat_starts)
    hc = mlstm_outputs(qc, kc, vc, lfc, igc, ctx_starts) if with_ctx_out else None
    return h, hc

def gla_states(k, v, loga, init):
    b = jnp.cumsum(loga, axis=-2)
    b_end = b[..., -1, :]
    s_loc = jnp.einsum('bhcld,bhcle->bhcde', k * jnp.exp(b_end[..., None, :] - b), v)

    def step(s, inp):
        be, sl = inp
        return jnp.exp(be)[..., None] * s + sl, s

    final, starts = lax.scan(step, init, (jnp.moveaxis(b_end, 2, 0), jnp.moveaxis(s_loc, 2, 0)))
    return jnp.moveaxis(starts, 0, 2), final

def gla_outputs(q, k, v, loga, s_start):
    ll = q.shape[-2]
    tri = jnp.tril(jnp.ones((ll, ll), dtype=bool))
    b = jnp.cumsum(loga, axis=-2)
    ref = b[..., ll // 2, :][..., None, :]
    att = jnp.einsum('bhctd,bhcsd->bhcts', q * jnp.exp(b - ref), k * jnp.exp(ref - b))
    att = jnp.where(tri, att, 0.0)
    return (jnp.einsum('bhcts,bhcse->bhcte', att, v)
            + jnp.einsum('bhctd,bhcde->bhcte', q * jnp.exp(b), s_start))

def gla_direction(lat, ctx, with_ctx_out):
    q, k, v, la = lat
    qc, kc, vc, lac = ctx
    bz, hh = q.shape[:2]
    init = jnp.zeros((bz, hh, GLA_DK, GLA_DV), jnp.float32)
    ctx_starts, ctx_final = gla_states(kc, vc, lac, init)
    lat_starts, _ = gla_states(k, v, la, ctx_final)
    h = gla_outputs(q, k, v, la, lat_starts)
    hc = gla_outputs(qc, kc, vc, lac, ctx_starts) if with_ctx_out else None
    return h, hc

def ml_inputs(p, d):
    return [to_chunks(orient(t, d), ML_CHUNK)
            for t in (p['ml_q'], p['ml_k'], p['ml_v'], p['ml_lf'][:, :, d], p['ml_ig'][:, :, d])]

def gla_inputs(p, d):
    return [to_chunks(orient(t, d), GLA_CHUNK)
            for t in (p['gla_q'], p['gla_k'], p['gla_v'], p['gla_la'][:, :, d])]

def mix_out(ml_h, ml_o, gla_h, gla_r, ml_g, gla_g, w_out, dtype):
    ml = jax.nn.sigmoid(ml_o) * head_rms(ml_h, ml_g)
    gl = jax.nn.silu(gla_r) * head_rms(gla_h, gla_g)
    return (jnp.concatenate([ml, gl], axis=-1) @ w_out).astype(dtype)

def token_mixer(h_lat, h_ctx, w_in, conv_w, gate_b, lr_w2, alpha_b, ml_g, gla_g, w_out,
                with_ctx_out):
    lat = prep_mixers(h_lat @ w_in, conv_w, gate_b, lr_w2, alpha_b, True)
    ctx = prep_mixers(h_ctx @ w_in, conv_w, gate_b, lr_w2, alpha_b, False)
    ml_lat, ml_ctx, gla_lat, gla_ctx = [], [], [], []
    for d in range(2):
        h, hc = mlstm_direction(ml_inputs(lat, d), ml_inputs(ctx, d), with_ctx_out)
        ml_lat.append(orient(from_chunks(h), d))
        g, gc = gla_direction(gla_inputs(lat, d), gla_inputs(ctx, d), with_ctx_out)
        gla_lat.append(orient(from_chunks(g), d))
        if with_ctx_out:
            ml_ctx.append(orient(from_chunks(hc), d))
            gla_ctx.append(orient(from_chunks(gc), d))
    y = mix_out(ml_lat[0] + ml_lat[1], lat['ml_o'], gla_lat[0] + gla_lat[1], lat['gla_r'],
                ml_g, gla_g, w_out, h_lat.dtype)
    yc = None
    if with_ctx_out:
        yc = mix_out(ml_ctx[0] + ml_ctx[1], ctx['ml_o'], gla_ctx[0] + gla_ctx[1], ctx['gla_r'],
                     ml_g, gla_g, w_out, h_ctx.dtype)
    return y, yc

def peer_ffn(h, wq, keys, u_tab, v_tab):
    bz, n, d = h.shape
    blocks = h.reshape(bz * n // PEER_BLOCK, PEER_BLOCK, d)

    def retrieve(xb):
        q = (xb @ wq).reshape(PEER_BLOCK, PEER_HEADS, 2, PEER_QDIM // 2)
        s = jnp.einsum('tphq,phkq->tphk', q, keys)
        top_s, top_i = lax.top_k(s, PEER_TOPK)
        cand = top_s[:, :, 0, :, None] + top_s[:, :, 1, None, :]
        best_s, best_c = lax.top_k(cand.reshape(PEER_BLOCK, PEER_HEADS, PEER_TOPK * PEER_TOPK),
                                   PEER_TOPK)
        i1 = jnp.take_along_axis(top_i[:, :, 0], best_c // PEER_TOPK, axis=-1)
        i2 = jnp.take_along_axis(top_i[:, :, 1], best_c % PEER_TOPK, axis=-1)
        idx = i1 * PEER_NKEYS + i2
        g = jax.nn.softmax(best_s.astype(jnp.float32), axis=-1).astype(xb.dtype)
        act = jax.nn.gelu(jnp.einsum('tpkd,td->tpk', u_tab[idx], xb), approximate=False)
        return jnp.einsum('tpk,tpkd->td', g * act, v_tab[idx])

    return lax.map(retrieve, blocks).reshape(bz, n, d)

def second_inputs(seed: int = 0) -> dict:
    key = jax.random.key(seed)
    ks = jax.random.split(key, 24)

    def nrm(k, shape, scale):
        return jax.random.normal(k, shape, jnp.float32) * scale

    f_bias = jnp.linspace(3.0, 6.0, ML_HEADS, dtype=jnp.float32)
    i_part = nrm(ks[8], (DEPTH, 2, 1, ML_HEADS), 0.1)
    f_part = f_bias + nrm(ks[9], (DEPTH, 2, 1, ML_HEADS), 0.1)
    ml_gate_b = jnp.concatenate([i_part, f_part], axis=2).reshape(DEPTH, 4 * ML_HEADS)
    return {
        'x': nrm(ks[0], (BATCH, SEQ, D_MODEL), 1.0),
        'c': nrm(ks[1], (BATCH, D_MODEL), 1.0),
        'ctx': nrm(ks[2], (BATCH, CTX_LEN, D_MODEL), 1.0),
        'c_ctx': nrm(ks[3], (D_MODEL,), 1.0),
        'w_mod': nrm(ks[4], (DEPTH, D_MODEL, 6 * D_MODEL), 0.5 * D_MODEL ** -0.5),
        'b_mod': nrm(ks[5], (DEPTH, 6 * D_MODEL), 0.02),
        'norm1_g': 1.0 + nrm(ks[6], (DEPTH, D_MODEL), 0.02),
        'w_in': nrm(ks[7], (DEPTH, D_MODEL, P_TOTAL), D_MODEL ** -0.5),
        'ml_conv_w': nrm(ks[10], (DEPTH, CONV_W, 2 * ML_WIDTH), CONV_W ** -0.5),
        'ml_gate_b': ml_gate_b,
        'ml_norm_g': 1.0 + nrm(ks[11], (DEPTH, ML_WIDTH), 0.02),
        'gla_lr_w2': nrm(ks[12], (DEPTH, 2, GLA_RANK, GLA_KEY_WIDTH), GLA_RANK ** -0.5),
        'gla_alpha_b': nrm(ks[13], (DEPTH, 2, GLA_KEY_WIDTH), 0.1),
        'gla_norm_g': 1.0 + nrm(ks[14], (DEPTH, GLA_WIDTH), 0.02),
        'w_out': nrm(ks[15], (DEPTH, MIX_WIDTH_2, D_MODEL), MIX_WIDTH_2 ** -0.5),
        'norm2_g': 1.0 + nrm(ks[16], (DEPTH, D_MODEL), 0.02),
        'peer_wq': nrm(ks[17], (DEPTH, D_MODEL, PEER_HEADS * PEER_QDIM), D_MODEL ** -0.5),
        'peer_keys': nrm(ks[18], (DEPTH, PEER_HEADS, 2, PEER_NKEYS, PEER_QDIM // 2),
                         (PEER_QDIM // 2) ** -0.5),
        'peer_u': nrm(ks[19], (DEPTH, PEER_EXPERTS, D_MODEL), D_MODEL ** -0.5),
        'peer_v': nrm(ks[20], (DEPTH, PEER_EXPERTS, D_MODEL), PEER_HEADS ** -0.5),
        'norm_f_g': 1.0 + nrm(ks[21], (D_MODEL,), 0.02),
    }

def second_block(x, c, ctx, c_ctx, w_mod, b_mod, norm1_g, w_in, ml_conv_w, ml_gate_b, ml_norm_g,
              gla_lr_w2, gla_alpha_b, gla_norm_g, w_out, norm2_g, peer_wq, peer_keys, peer_u,
              peer_v, norm_f_g):
    cond = jax.nn.silu(c)
    cond_ctx = jax.nn.silu(c_ctx)
    for layer in range(DEPTH):
        update_ctx = layer + 1 < DEPTH
        mod = (cond @ w_mod[layer] + b_mod[layer])[:, None, :]
        mod_c = cond_ctx @ w_mod[layer] + b_mod[layer]
        sh1, sc1, g1, sh2, sc2, g2 = jnp.split(mod, 6, axis=-1)
        csh1, csc1, cg1, csh2, csc2, cg2 = jnp.split(mod_c, 6, axis=-1)

        h = rms_norm_2(x, norm1_g[layer]) * (1.0 + sc1) + sh1
        hc = rms_norm_2(ctx, norm1_g[layer]) * (1.0 + csc1) + csh1
        y, yc = token_mixer(h, hc, w_in[layer], ml_conv_w[layer], ml_gate_b[layer],
                            gla_lr_w2[layer], gla_alpha_b[layer], ml_norm_g[layer],
                            gla_norm_g[layer], w_out[layer], update_ctx)
        x = x + g1 * y
        h2 = rms_norm_2(x, norm2_g[layer]) * (1.0 + sc2) + sh2
        x = x + g2 * peer_ffn(h2, peer_wq[layer], peer_keys[layer], peer_u[layer], peer_v[layer])

        if update_ctx:
            ctx = ctx + cg1 * yc
            hc2 = rms_norm_2(ctx, norm2_g[layer]) * (1.0 + csc2) + csh2
            ctx = ctx + cg2 * peer_ffn(hc2, peer_wq[layer], peer_keys[layer], peer_u[layer],
                                       peer_v[layer])
    return rms_norm_2(x, norm_f_g)


def setup_inputs(seed=0):
    out = dict(first_inputs(seed))
    for name, value in second_inputs(seed + 1).items():
        if name != "x":
            out[name + "_2"] = value
    return out


def reference(
    x, mem, norm_mix_g, w_in, sb_q_norm_g, sb_k_norm_g, conv_dw_w, conv_dw_b, conv_ln_g,
    conv_ln_b, conv_pw2_w, ssm_lam_re, ssm_lam_im, ssm_log_dt, ssm_b_re, ssm_b_im, ssm_c_re,
    ssm_c_im, ssm_d, ssm_glu_w, branch_norm_g, w_out, norm_xa_g, norm_mem_g, xa_wq, xa_wk,
    xa_wv, xa_q_norm_g, xa_k_norm_g, xa_wo, norm_ffn_g, ffn_w_in, ffn_w_out, c_2, ctx_2,
    c_ctx_2, w_mod_2, b_mod_2, norm1_g_2, w_in_2, ml_conv_w_2, ml_gate_b_2, ml_norm_g_2,
    gla_lr_w2_2, gla_alpha_b_2, gla_norm_g_2, w_out_2, norm2_g_2, peer_wq_2, peer_keys_2,
    peer_u_2, peer_v_2, norm_f_g_2,
):
    x = first_block(
        x, mem, norm_mix_g, w_in, sb_q_norm_g, sb_k_norm_g, conv_dw_w, conv_dw_b, conv_ln_g,
        conv_ln_b, conv_pw2_w, ssm_lam_re, ssm_lam_im, ssm_log_dt, ssm_b_re, ssm_b_im, ssm_c_re,
        ssm_c_im, ssm_d, ssm_glu_w, branch_norm_g, w_out, norm_xa_g, norm_mem_g, xa_wq, xa_wk,
        xa_wv, xa_q_norm_g, xa_k_norm_g, xa_wo, norm_ffn_g, ffn_w_in, ffn_w_out,
    )
    return second_block(
        x, c_2, ctx_2, c_ctx_2, w_mod_2, b_mod_2, norm1_g_2, w_in_2, ml_conv_w_2, ml_gate_b_2,
        ml_norm_g_2, gla_lr_w2_2, gla_alpha_b_2, gla_norm_g_2, w_out_2, norm2_g_2, peer_wq_2,
        peer_keys_2, peer_u_2, peer_v_2, norm_f_g_2,
    )


_drawn_inputs = setup_inputs


def setup_inputs(seed=0):
    import zlib

    import numpy as np

    out = dict(_drawn_inputs(seed))
    spreads = {}
    factors = {'norm_mix_g': 3.025,
     'sb_q_norm_g': 8.0,
     'sb_k_norm_g': 8.0,
     'conv_dw_b': 2.975,
     'conv_ln_g': 5.95,
     'conv_ln_b': 6.282,
     'ssm_lam_re': 8.0,
     'ssm_b_re': 2.695,
     'ssm_c_re': 2.701,
     'branch_norm_g': 3.648,
     'norm_xa_g': 8.0,
     'norm_mem_g': 8.0,
     'xa_q_norm_g': 8.0,
     'xa_k_norm_g': 8.0,
     'norm_ffn_g': 4.634,
     'ctx_2': 2.835,
     'b_mod_2': 4.27,
     'norm1_g_2': 8.0,
     'ml_norm_g_2': 200.0,
     'gla_lr_w2_2': 2.88,
     'gla_alpha_b_2': 21.824,
     'gla_norm_g_2': 41.558,
     'norm2_g_2': 64.0,
     'norm_f_g_2': 24.328,
     'c_ctx_2': 2.979,
     'ml_conv_w_2': 8.0}
    for name, (base, spread) in spreads.items():
        noise = np.random.default_rng([zlib.crc32(name.encode()), seed]).standard_normal(out[name].shape)
        drawn = base * np.exp(spread * noise) if base else spread * noise
        out[name] = jnp.asarray(drawn.astype(out[name].dtype))
    for name, factor in factors.items():
        out[name] = (out[name] * factor).astype(out[name].dtype)
    return out
```

```python
from contextlib import ExitStack

import concourse.bass as bass
from concourse import mybir

ALU = mybir.AluOpType
ACT = mybir.ActivationFunctionType
AX = mybir.AxisListType
F32 = mybir.dt.float32
F32R = mybir.dt.float32r
U32 = mybir.dt.uint32
I32 = mybir.dt.int32

P = 128
D = 1024
KD = D // P
T = 256
TB = T // P
EPS = 1e-6
RING, SLOT = 6, 2048
BANKS = 4
SB_H, SB_D = 8, 64
SB_SCALE = SB_D ** -0.5
CW = 31
CLIP = 30.0
NEVER = -1e30
NS = 8
MAGIC = 12582912.0
PI_A, PI_B, PI_C = 6.28125, 0.0019350051879882812, 3.0199160505563e-07
TURN = 6.2831845
XH, XD = 4, 256
FH = 2816
FB = FH // P
MH = 4
GC = 64
NE = 128
PH, TOPK = 8, 16

COLS = {}
_at = 0
for _name, _n in (
    ("mix_g", 8), ("sbq_g", 1), ("sbk_g", 1), ("dw_w", 2 * CW), ("dw_b", 2), ("ln_g", 2), ("ln_b", 2),
    ("lam_re", NS), ("lam_im", NS), ("log_dt", NS), ("ssm_d", 2), ("branch_g", 8), ("xa_g", 8), ("mem_g", 8),
    ("xaq_g", 2), ("xak_g", 2), ("ffn_g", 8), ("c", 8), ("c_ctx", 8), ("b_mod", 48), ("norm1_g", 8),
    ("conv_w", 24), ("ig_b", 1), ("f_b", 1), ("ml_g", 4), ("alpha_b", 4), ("gla_g", 4), ("norm2_g", 8), ("normf_g", 8),
):
    COLS[_name] = (_at, _n)
    _at += _n
NPAR = _at


class Products:

    def __init__(self):
        self.number, self.bank, self.takers, self.rank = {}, {}, {}, {}
        self.count, self.turn = 0, 0
        self.takes = {}
        self.in_bank = [None] * BANKS

    def add(self, key, takers, banked=True):
        assert key not in self.number, key
        self.number[key] = self.count
        self.count += 1
        self.takers[key] = takers
        before = None
        if banked:
            b = self.turn % BANKS
            self.turn += 1
            before, self.in_bank[b] = self.in_bank[b], key
            self.bank[key] = b
        for r in takers:
            self.takes[r] = self.takes.get(r, 0) + 1
            self.rank[key, r] = self.takes[r]
        return before


class Area:

    def __init__(self, ap, size):
        self.ap, self.size, self.at, self.top = ap, size, 0, 0

    def take(self, *shape, parts=P, dt=None):
        n = 1
        for s in shape:
            n *= s
        a = self.ap[0:parts, self.at:self.at + n]
        self.at += n
        assert self.at <= self.size, (self.at, self.size)
        if dt is not None:
            a = a.bitcast(dt)
        names = "abcde"[:len(shape)]
        if len(shape) > 1:
            a = a.rearrange(f"p ({' '.join(names)}) -> p {' '.join(names)}", **{n: s for n, s in zip(names, shape)})
        return a


def program(nc, d):
    plan = Products()
    items, released = [], []

    with ExitStack() as ctx:
        def sb(name, shape, dt=F32):
            t = ctx.enter_context(nc.sbuf_tensor(name, shape, dt))
            return t[tuple(slice(0, n) for n in shape)]

        def sem(name):
            return ctx.enter_context(nc.semaphore(name))

        x = sb("x", [P, KD, T])
        par = sb("par", [P, NPAR])
        ones = sb("ones", [P, P])
        eps = sb("eps", [P, 1])
        mod = sb("mod", [P, 6, KD, 2])
        gain = sb("gain", [P, 3, KD])
        big = sb("big", [P, NE * T])
        shapes = {"ring": [P, RING, SLOT], "hh": [P, 2, KD, T], "tables": [P, 2, P], "idx": [P, 3, T]}

        def views(prefix, dt):
            with ExitStack() as place:
                handles = {n: place.enter_context(nc.sbuf_tensor(prefix + n, shape, dt)) for n, shape in shapes.items()}
            return {n: t[tuple(slice(0, w) for w in shapes[n])] for n, t in handles.items()}

        whole, split = views("", F32), views("split_", F32R)
        ring = whole["ring"]
        hh = whole["hh"]
        other, h = hh[:, 0], hh[:, 1]
        tables = whole["tables"]
        ident, iota = tables[:, 0], tables[:, 1]
        idx = whole["idx"]
        ps = ctx.enter_context(nc.psum_tensor("ps", [P, 8, 512], F32))
        sums = ps[:, 4:8, :].rearrange("p b (h t) -> p (b h) t", t=T)

        def col(name, i=0, parts=P):
            at, n = COLS[name]
            assert i < n
            return par[0:parts, at + i:at + i + 1]

        def cols(name):
            at, n = COLS[name]
            return par[:, at:at + n]

        area = Area(big, NE * T)
        sq = area.take(KD, T)
        std = area.take(2, 512)
        cond = area.take(KD, 2)
        first = area.at
        lower = area.take(P)
        pair1 = area.take(P)
        qk = area.take(8, T)
        v_sb = area.take(TB, 512)
        u = area.take(2, T)
        glu_e = area.take(2, T)
        pad = area.take(2, CW - 1 + T)
        conv = area.take(2, T)
        cvo = area.take(2, T)
        ssb = area.take(4, NS, 16)
        sm = area.take(24, NS)
        bb = area.take(2, 2, 4, 32)
        bb_t = area.take(2, 2, P)
        bbt = area.take(2, NS, 16)
        cc = area.take(3, NS, 32)
        ramp = area.take(T)
        trig = area.take(2, NS, T)
        bu = area.take(2, NS, T)
        rot = area.take(2, NS, T)
        rot2 = area.take(NS, T)
        ys = area.take(2, T)
        g_e = area.take(2, T)
        mixed = area.take(8, T)
        mixer_end = area.at
        area.at = first + 0
        sbz = trig.rearrange("p a b t -> p (a b t)")
        z_s = sbz[:, 0:768].rearrange("p (a t) -> p a t", a=2)
        z_e = sbz[:, 768:1536].rearrange("p (a t) -> p a t", a=2)
        z_p = sbz[:, 1536:2304].rearrange("p (a t) -> p a t", a=2)
        z_w = sbz[:, 2304:3840].rearrange("p (a t) -> p a t", a=4)
        area.at = first
        xk = area.take(8, T)
        xv = area.take(2, D)
        xq = area.take(8, T)
        xp = area.take(2, 2, T)
        xpt = area.take(2, 2, T)
        xo = area.take(8, T)
        xs = area.take(XH, 8)
        area.at = first
        hid = area.take(FB, T)
        f_e = area.take(2, T)
        f_t = area.take(2, T)

        area.at = first
        mk_t = area.take(MH, 2 * T)
        mq_t = area.take(MH, T)
        raw = area.take(2 * MH * 512)
        mk_raw = raw[:, 0:MH * 512].rearrange("p (a t) -> p a t", a=MH)
        mq_raw = raw[:, MH * 512:MH * 768].rearrange("p (a t) -> p a t", a=MH)
        dec = raw.rearrange("p (e d s t) -> p e d s t", e=2, d=2, s=4)
        dec_sq = raw[:, 0:2048].rearrange("p (a t) -> p a t", a=8)
        q_z = raw[:, 0:2048].rearrange("p (j i t) -> p j i t", j=2, i=4)
        att = area.ap[:, first:first + MH * 512].rearrange("p (j d b h t) -> p j d b h t", j=2, d=2, b=2, h=2)
        out_g = raw[:, 2048:4096].rearrange("p (a t) -> p a t", a=8)
        mv = area.take(4, 512)
        gv = area.take(4, 512)
        la = area.take(4, 512)
        cs = area.take(4, 512)
        gk_t = area.take(2, 512)
        gq_t = area.take(2, T)
        q_in = area.take(4, T)
        k_in = area.take(4, T)
        q_st = area.take(4, T)
        late = area.at
        kd_t = area.take(4, 4, P)
        st = area.take(4, 5, P)
        area.at = max(area.at, late + 10 * 512)
        rows2_at = area.at
        rows2 = area.take(2, T)[0:36]
        gcol = area.take(4, 36)
        e_end = area.take(4, 8)
        floor = area.take(2, 2, T)
        mix2 = area.take(8, T)
        mlh, glh = mix2[:, 0:4], mix2[:, 4:8]
        after_all = area.at
        area.at = late
        g_rows = area.take(6, 512)[0:36]
        glr = area.take(512)[0:32]
        lr_w = area.take(2, T)[0:32]
        reset = area.take(2, 512)
        assert area.at <= rows2_at, (area.at, rows2_at)
        area.at = first
        pq = area.take(2 * PH, T)
        psc = area.take(TB, 2 * PH, NE)
        psc2 = area.take(2, NE)
        tv = area.take(TB, PH, 2, TOPK)
        ti = area.take(TB, PH, 2, TOPK, dt=U32)
        tf = area.take(TB, PH, 2, TOPK)
        cand = area.take(PH, TOPK, TOPK)
        cand2 = area.take(TOPK * TOPK)
        bv = area.take(TB, PH, TOPK)
        bi = area.take(TB, PH, TOPK, dt=U32)
        side = area.take(2, TB, PH, TOPK, dt=U32)
        side_f = area.take(2, TB, PH, TOPK)
        hit = area.take(PH, TOPK, TOPK)
        keys3 = area.take(3, TB, PH, TOPK)
        bsum = area.take(TB, PH)
        g_all = big.rearrange("p (t e) -> p t e", e=NE)
        half_slots = ring.rearrange("p s (n w) -> p (s n) w", n=2)
        hot = half_slots[:, 8:10, :].rearrange("p a w -> p (a w)").rearrange("p (n s e) -> p n s e", n=8, s=2)
        u_tile, v_tile = half_slots[:, 0:4, :], half_slots[:, 4:8, :]
        split_slots = split["ring"].rearrange("p s (n w) -> p (s n) w", n=2)
        u_high, v_high = split_slots[:, 8:10, :], split_slots[:, 10:12, :]
        u_low, v_low = split_slots[:, 0:4, :], split_slots[:, 4:8, :]
        h_high, h_low = split["hh"][:, 0], split["hh"][:, 1]
        act_e = idx[:, 0:2, :]
        w_low = split["idx"][:, 0:2, :]
        w_high = [split["idx"][:, 2, :], split["tables"].rearrange("p a b -> p (a b)")]
        std_f = idx[:, 0, :]
        loaded = sem("inputs_loaded")
        in_ring = [sem(f"weights_in_slot{i}") for i in range(RING)]
        made = sem("product_made")
        drained = {"dve": sem("products_taken_by_vector"), "act": sem("products_taken_by_scalar")}
        chain = {n: sem(f"{n}_step_done") for n in ("dve", "act", "pool")}
        flags = {}

        def flag(name):
            if name not in flags:
                flags[name] = sem(name)
            return flags[name]

        def number(key):
            return plan.number[key] + 1

        def emptied(slot):
            return released[max(n for n in range(len(items)) if n % RING == slot)]

        class Steps:

            def __init__(self, eng, name):
                self.eng, self.name, self.n = eng, name, 0
                self.taken = 0

            def link(self, ins):
                self.n += 1
                ins.then_inc(chain[self.name], 1)
                self.eng.wait_ge(chain[self.name], self.n)

            def product(self, key):
                self.eng.wait_ge(made, number(key))
                return ps[:, plan.bank[key], :]

            def took(self, key, ins):
                self.taken += 1
                assert plan.rank[key, self.name] == self.taken, key
                ins.then_inc(drained[self.name], 1)

            def after(self, key, taker=None):
                for r in ([taker] if taker else plan.takers[key]):
                    self.eng.wait_ge(drained[r], plan.rank[key, r])

            def wait(self, name, n=1):
                self.eng.wait_ge(flag(name), n)

        block = ctx.enter_context(nc.Block())

        @block.tensor
        def _(pe):
            open_items = []

            def after(key, taker=None):
                for r in ([taker] if taker else plan.takers[key]):
                    pe.wait_ge(drained[r], plan.rank[key, r])

            def begin(key, *takers):
                before = plan.add(key, takers)
                if before is not None:
                    after(before)
                return ps[:, plan.bank[key], :]

            def weights(name, i, width=SLOT):
                n = len(items)
                items.append((name, i, width))
                released.append(None)
                open_items.append(n)
                pe.wait_ge(in_ring[n % RING], 16 * (n // RING + 1))
                return ring[:, n % RING, 0:width]

            def release():
                for n in open_items:
                    released[n] = plan.count
                open_items.clear()

            def mm(out, lhsT, rhs, start=True, stop=True):
                return nc.tensor.matmul(out, lhsT, rhs, start=start, stop=stop, skip_group_check=True)

            def project(key, takers, name, i, rhs, nk=KD, halves=2, n=T):
                bank = begin(key, *takers)
                w = weights(name, i, halves * nk * P).rearrange("p (m k c) -> p m k c", m=halves, k=nk)
                for m in range(halves):
                    for k in range(nk):
                        last = mm(bank[:, m * n:(m + 1) * n], w[:, m, k, :], rhs(k), k == 0, k == nk - 1)
                last.then_inc(made, 1)
                release()

            def total(key, parts, takers=("act",), n=T, ones_=None):
                bank = begin(key, *takers)
                for i, part in enumerate(parts):
                    last = mm(bank[:, 0:n], ones if ones_ is None else ones_, part, i == 0, i == len(parts) - 1)
                last.then_inc(made, 1)

            def tokens(key, takers, w, act, block_):
                bank = begin(key, *takers)
                for k in range(KD):
                    last = mm(bank, act[:, k, block_ * P:(block_ + 1) * P], w[k // 4][:, k % 4, :], k == 0, k == KD - 1)
                last.then_inc(made, 1)

            hk = lambda k: h[:, k, :]
            ok = lambda k: other[:, k, :]

            pe.wait_ge(flag("constants_ready"), 5)
            pe.wait_ge(flag("squares_ready"), 1)
            total("mix_sum", [sq[:, k, :] for k in range(KD)])
            pe.wait_ge(flag("h_ready"), 1)
            project("u", ("dve",), "w_in", 8, hk)
            project("conv_b", ("act",), "w_in", 7, hk)
            project("conv_a", ("dve",), "w_in", 6, hk)
            wv = [weights("w_in_v", i).rearrange("p (k n) -> p k n", k=4) for i in range(2)]
            for b in range(TB):
                tokens(("v", b), ("act",), wv, h, b)
            release()
            for i in range(4):
                project(("qk", i), ("act",), "w_in", i, hk)
            pe.wait_ge(flag("b_ready"), 1)
            bank = begin("b_t", "act")
            for i in range(4):
                last = nc.tensor.transpose(bank[:, i * P:(i + 1) * P],
                                           bb[:, i // 2, i % 2, :, :].rearrange("p c h -> p (c h)"), ident[:, :])
            last.then_inc(made, 1)
            after("b_t")
            after("u")
            for c in range(NS):
                bank = begin(("bu", c), "act")
                rows = slice(32 * (c % 4), 32 * (c % 4) + 32)
                for i in range(2):
                    last = mm(bank[:, i * T:(i + 1) * T], bb_t[rows, i, c // 4, :], u[rows, c // 4, :])
                last.then_inc(made, 1)
            pe.wait_ge(flag("squares_ready"), 2)
            for i in range(4):
                bank = begin(("qk_sum", i), "act")
                for j in range(2):
                    last = mm(bank[:, j * T:(j + 1) * T], pair1, sq[:, 2 * i + j, :])
                last.then_inc(made, 1)
            pe.wait_ge(flag("cond_ready"), 1)
            for g in range(6):
                bank = begin(("mod", g), "dve")
                for i in range(4):
                    w = weights("w_mod", 4 * g + i).rearrange("p (m k c) -> p m k c", m=2, k=KD)
                    for m in range(2):
                        for k in range(KD):
                            at = 4 * i + 2 * m
                            last = mm(bank[:, at:at + 2], w[:, m, k, :], cond[:, k, :], k == 0, k == KD - 1)
                last.then_inc(made, 1)
                release()
            pe.wait_ge(flag("states_ready"), 1)
            bank = begin("ssm_y", "dve")
            for c in range(NS):
                rows = slice(32 * (c % 4), 32 * (c % 4) + 32)
                out = bank[rows, (c // 4) * T:(c // 4 + 1) * T]
                mm(out, cc[:, 0, c, :], bu[:, 0, c, :], True, False)
                last = mm(out, cc[:, 2, c, :], bu[:, 1, c, :], False, True)
            last.then_inc(made, 1)
            after("ssm_y")
            wg = weights("ssm_glu", 0, 1024).rearrange("p (m k c) -> p m k c", m=4, k=2)
            for i, (key, taker) in enumerate((("glu_b", "act"), ("glu_a", "dve"))):
                bank = begin(key, taker)
                for m in range(2):
                    for k in range(2):
                        last = mm(bank[:, m * T:(m + 1) * T], wg[:, 2 - 2 * i + m, k, :], ys[:, k, :], k == 0, k == 1)
                last.then_inc(made, 1)
            release()
            pe.wait_ge(flag("taps_done"), 2 * CW)
            total("ln_mean", [conv[:, i, :] for i in range(2)], takers=("dve",))
            pe.wait_ge(flag("conv_squares_ready"), 1)
            total("ln_var", [glu_e[:, i, :] for i in range(2)])
            pe.wait_ge(flag("conv_ready"), 1)
            project("pw2", ("dve",), "conv_pw2", 0, lambda k: conv[:, k, :], nk=2)
            pe.wait_ge(flag("qk_scaled"), 4)
            after(("v", 1))

            def scores(hd):
                rows = slice(64 * (hd % 2), 64 * (hd % 2) + 64)
                bank = begin(("z", hd), "dve")
                mm(bank[:, 0:T], qk[rows, 4 + hd // 2, 0:P], qk[rows, hd // 2, :])
                mm(bank[:, T:T + P], qk[rows, 4 + hd // 2, P:T], qk[rows, hd // 2, P:T]).then_inc(made, 1)

            def later(hd):
                pe.wait_ge(flag("softplus_ready"), 2 * (hd + 1))
                s = z_p[:, hd % 2, :]
                bank = begin(("later", hd), "dve")
                mm(bank[:, 0:T], lower, s[:, 0:T], True, False)
                mm(bank[:, P:T], ones, s[:, T:T + P], False, True)
                mm(bank[:, T:T + P], lower, s[:, T:T + P]).then_inc(made, 1)

            def weighted(pair):
                bank = begin(("o", pair), "act")
                for hd in (2 * pair, 2 * pair + 1):
                    pe.wait_ge(flag("sb_weights_ready"), hd + 1)
                    out = bank[64 * (hd % 2):64 * (hd % 2) + 64, :]
                    w = z_w[:, hd % 4, :]
                    vh = slice(SB_D * hd, SB_D * hd + SB_D)
                    mm(out[:, 0:T], v_sb[:, 0, vh], w[:, 0:T], True, False)
                    last = mm(out[:, P:T], v_sb[:, 1, vh], w[:, T:T + P], False, True)
                last.then_inc(made, 1)

            scores(0)
            scores(1)
            for pair in range(SB_H // 2):
                for hd in (2 * pair, 2 * pair + 1):
                    later(hd)
                    if hd + 2 < SB_H:
                        scores(hd + 2)
                if pair:
                    weighted(pair - 1)
            weighted(SB_H // 2 - 1)
            pe.wait_ge(flag("branch_squares_ready"), 1)
            total("ssm_sum", [sq[:, 6 + i, :] for i in range(2)])
            pe.wait_ge(flag("branch_squares_ready"), 2)
            total("conv_sum", [sq[:, 4 + i, :] for i in range(2)])
            pe.wait_ge(flag("branch_squares_ready"), 3)
            total("sb_sum", [sq[:, i, :] for i in range(4)])
            pe.wait_ge(flag("mixed_ready"), 3)
            for i in range(4):
                project(("mix_out", i), ("dve",), "w_out", i, lambda k: mixed[:, k, :])
            pe.wait_ge(flag("squares_ready"), 3)
            total("mem_sum", [sq[:, k, :] for k in range(KD)])
            pe.wait_ge(flag("squares_ready"), 4)
            total("xa_sum", [sq[:, k, :] for k in range(KD)])
            pe.wait_ge(flag("other_ready"), 1)
            for i in range(4):
                project(("xk", i), ("act",), "xa_wk", i, ok)
            for n in range(2):
                wv = [weights("xa_wv", 2 * n + i).rearrange("p (k n) -> p k n", k=4) for i in range(2)]
                for b in range(TB):
                    tokens(("xv", n, b), ("act",), wv, other, b)
                release()
            pe.wait_ge(flag("squares_ready"), 5)
            for hd in range(XH):
                total(("xk_sum", hd), [sq[:, 2 * hd + j, :] for j in range(2)])
            pe.wait_ge(flag("h_ready"), 2)
            for i in range(4):
                project(("xq", i), ("act",), "xa_wq", i, hk)
            pe.wait_ge(flag("squares_ready"), 6)
            for hd in range(XH):
                total(("xq_sum", hd), [sq[:, 2 * hd + j, :] for j in range(2)])
            after(("xv", 1, 1))

            def xa_scores(hd):
                pe.wait_ge(flag("xa_heads_ready"), hd + 1)
                bank = begin(("xs", hd), "dve", "act")
                for b in range(TB):
                    for j in range(2):
                        last = mm(bank[:, b * T:(b + 1) * T], xq[:, 2 * hd + j, b * P:(b + 1) * P], xk[:, 2 * hd + j, :],
                                  j == 0, j == 1)
                last.then_inc(made, 1)

            xa_scores(0)
            for hd in range(XH):
                if hd + 1 < XH:
                    xa_scores(hd + 1)
                pe.wait_ge(flag("xa_probs_ready"), hd + 1)
                bank = begin(("xpt", hd), "act")
                for m in range(2):
                    for b in range(TB):
                        at = m * T + b * P
                        last = nc.tensor.transpose(bank[:, at:at + P], xp[:, hd % 2, b, m * P:(m + 1) * P], ident[:, :])
                last.then_inc(made, 1)
                after(("xpt", hd))
                bank = begin(("xo", hd), "dve")
                for j in range(2):
                    for m in range(2):
                        last = mm(bank[:, j * T:(j + 1) * T], xv[:, m, XD * hd + P * j:XD * hd + P * (j + 1)],
                                  xpt[:, hd % 2, m, :], m == 0, m == 1)
                last.then_inc(made, 1)
            after(("xo", XH - 1))
            for i in range(4):
                project(("xa_out", i), ("dve",), "xa_wo", i, lambda k: xo[:, k, :])
            pe.wait_ge(flag("squares_ready"), 7)
            total("ffn_sum", [sq[:, k, :] for k in range(KD)])
            pe.wait_ge(flag("squares_ready"), 8)
            total("ctx_sum", [sq[:, k, :] for k in range(KD)])
            pe.wait_ge(flag("h_ready"), 3)
            for j in range(FB):
                project(("ffn", j), ("act", "dve"), "ffn_in", j, hk)
            for j in range(FB // 2):
                w = weights("ffn_out", j).rearrange("p (k c) -> p k c", k=2)
                for i in range(2):
                    after(("ffn", 2 * j + i), "dve")
                    for m in range(KD):
                        last = mm(sums[:, m, :], w[:, i, m * P:(m + 1) * P], hid[:, 2 * j + i, :],
                                  j == 0 and i == 0 and m % 2 == 0, j == FB // 2 - 1 and i == 1)
                plan.add(("ffn_out", j), ("dve",) if j == FB // 2 - 1 else (), banked=False)
                last.then_inc(made, 1)
                release()
            pe.wait_ge(flag("squares_ready"), 9)
            total("lat_sum", [sq[:, k, :] for k in range(KD)])
            pe.wait_ge(flag("other_ready"), 2)
            pe.wait_ge(flag("h_ready"), 4)

            def both(key, taker, w, m=P):
                bank = begin(key, taker)
                for k in range(KD):
                    last = mm(bank[0:m, :].rearrange("p (a t) -> p a t", a=2), w[:, k, :], hh[:, :, k, :], k == 0, k == KD - 1)
                last.then_inc(made, 1)

            w = weights("gates", 0, KD * 104).rearrange("p (k c) -> p k c", k=KD)
            both("ig", "act", w[:, :, 0:36], 36)
            both("fg", "dve", w[:, :, 36:72], 36)
            both("glr", "act", w[:, :, 72:104], 32)
            release()
            for key, name in (("mk", "mk"), ("gk", "gk")):
                for i in range(2 if key == "mk" else 1):
                    w = weights("w2_" + name, i).rearrange("p (m k c) -> p m k c", m=2, k=KD)
                    for m in range(2):
                        both((key, 2 * i + m), "act", w[:, m])
                    release()
            for i in range(2):
                project(("mq", i), ("act",), "w2_mq", i, hk)
            project("gq", ("act",), "w2_gq", 0, hk)
            after("glr")
            pe.wait_ge(flag("lr_loaded"), 16)
            for i in range(4):
                bank = begin(("alpha", i), "dve")
                mm(bank, lr_w[:, i // 2, (i % 2) * P:(i % 2) * P + P], glr).then_inc(made, 1)
            for name in ("mv", "gv"):
                wv = [weights("w2_" + name, i).rearrange("p (k n) -> p k n", k=4) for i in range(2)]
                for b in range(4):
                    tokens((name, b), ("act",), wv, other if b < 2 else h, b % 2)
                release()
            pe.wait_ge(flag("gate_rows_ready"), 1)
            bank = begin("gcol", "act")
            for b in range(4):
                last = nc.tensor.transpose(bank[:, 36 * b:36 * b + 36], g_rows[:, 3, b * P:(b + 1) * P], ident[0:36, 0:36])
            last.then_inc(made, 1)
            pe.wait_ge(flag("m_rows_ready"), 2)

            def similarities(hd):
                if hd == 0:
                    pe.wait_ge(flag("mkq_ready"), 2)
                for dr in range(2):
                    r = 32 * dr + hd
                    bank = begin(("row", hd, dr), "act", "dve")
                    mm(bank.rearrange("p (a t) -> p a t", a=2), ident[0:36, r:r + 1].to_broadcast([36, P]),
                       rows2).then_inc(made, 1)
                for seg in range(2):
                    bank = begin(("ms", hd, seg), "dve")
                    for b in range(2):
                        at = (2 * seg + b) * P
                        last = mm(bank[:, b * T:(b + 1) * T], mk_t[:, hd, at:at + P], mq_t[:, hd, :])
                    last.then_inc(made, 1)

            def values(hd):
                for dr in range(2):
                    if dr == 0:
                        pe.wait_ge(flag("scores_ready"), hd + 1)
                    else:
                        after(("ms", hd, 1))
                    bank = begin(("mn", hd, dr), "dve")
                    parts = [(0, 0), (1, 0), (2, 0), (3, P)] if dr == 0 else [(0, 0), (1, 0), (3, 0), (2, 0)]
                    for half in range(2):
                        for n, (b, lo) in enumerate(parts):
                            hi = P if (dr == 1 and b == 2) else T
                            w = ones if half else mv[:, b, hd * P:(hd + 1) * P]
                            last = mm(bank[:, half * T + lo:half * T + hi], w, dec[:, hd % 2, dr, b, lo:hi], n == 0, n == 3)
                    last.then_inc(made, 1)

            similarities(0)
            for hd in range(MH):
                if hd + 1 < MH:
                    similarities(hd + 1)
                values(hd)
            pe.wait_ge(flag("gla_ready"), 1)
            for i in range(4):
                bank = begin(("kd", i), "act")
                for b in range(4):
                    last = nc.tensor.transpose(bank[:, b * P:(b + 1) * P], la[:, i, b * P:(b + 1) * P], ident[:, :])
                last.then_inc(made, 1)
            pe.wait_ge(flag("gla_ready"), 2)
            for j in range(2):
                bank = begin(("att", j), "act")
                rows_ = slice(64 * j, 64 * j + 64)
                for c in range(4):
                    for dr in range(2):
                        for hp in range(2):
                            i = 2 * dr + hp
                            at = 256 * dr + 128 * (c // 2) + 64 * hp
                            last = mm(bank[64 * (c % 2):64 * (c % 2) + 64, at:at + 64], k_in[rows_, i, c * GC:(c + 1) * GC],
                                      q_in[rows_, i, c * GC:(c + 1) * GC])
                last.then_inc(made, 1)
            for i in range(4):
                after(("kd", i))
                for odd in ((1, 0) if i < 2 else (0, 1)):
                    bank = begin(("add", i, odd), "dve")
                    rows_ = slice(64 * odd, 64 * odd + 64)
                    for b in range(4):
                        for j in range(2):
                            hd = 2 * (i % 2) + j
                            last = mm(bank[64 * j:64 * j + 64, b * P:(b + 1) * P], kd_t[rows_, i, b, 64 * j:64 * j + 64],
                                      gv[rows_, b, hd * P:(hd + 1) * P])
                    last.then_inc(made, 1)
            pe.wait_ge(flag("att_ready"), 4)
            after(("add", 3, 1))
            pe.wait_ge(flag("q_split"), 1)
            for pair in range(2):
                bank = begin(("go", pair), "act")
                for j in range(2):
                    hd = 2 * pair + j
                    for b in range(2):
                        out = bank[:, j * T + b * P:j * T + (b + 1) * P]
                        for dr in range(2):
                            mm(out, gv[:, 2 + b, hd * P:(hd + 1) * P], att[:, j, dr, b, pair, :], dr == 0, False)
                            for c in (2 * b, 2 * b + 1):
                                at = (c % 2) * GC
                                last = mm(out[:, at:at + GC], st[:, 2 * dr + pair, c, :],
                                          q_z[:, j, 2 * dr + pair, c * GC:(c + 1) * GC], False, dr == 1)
                last.then_inc(made, 1)
            for name in ("mo", "gr"):
                for i in range(2):
                    project((name, i), ("act",), "w2_" + name, i, hk)
            pe.wait_ge(flag("squares_ready"), 10)
            for i in range(4):
                bank = begin(("mix2_sum", i), "act")
                mm(bank, ones, dec_sq[:, 2 * i:2 * i + 2, :].rearrange("p a t -> p (a t)")).then_inc(made, 1)
            pe.wait_ge(flag("mix2_ready"), 4)
            for i in range(4):
                project(("mix2_out", i), ("dve",), "w2_out", i, lambda k: mix2[:, k, :])
            pe.wait_ge(flag("squares_ready"), 11)
            total("peer_sum", [sq[:, k, :] for k in range(KD)])
            pe.wait_ge(flag("h_ready"), 5)
            for i in range(PH):
                project(("pq", i), ("act",), "peer_wq", i, hk)
            w = weights("peer_keys", 0).rearrange("p (s n) -> p s n", n=NE)
            for b in range(TB):
                for g in range(4):
                    bank = begin(("psc", b, g), "act")
                    for j in range(4):
                        if b == 0:
                            after(("pq", (4 * g + j) // 2))
                        last = mm(bank[:, j * NE:(j + 1) * NE], pq[:, 4 * g + j, b * P:(b + 1) * P], w[:, 4 * g + j, :])
                    last.then_inc(made, 1)
            release()
            for b in range(TB):
                pe.wait_ge(flag("picked"), b + 1)
                bank = begin(("keys3", b), "act")
                for i in range(3):
                    last = nc.tensor.transpose(bank[:, i * P:(i + 1) * P], keys3[:, i, b].rearrange("p h k -> p (h k)"), ident[:, :])
                last.then_inc(made, 1)
            after(("keys3", 0))
            after(("keys3", 1))
            hot_ready, w_made, w_read = flag("one_hot_ready"), flag("expert_weights_made"), flag("expert_weights_read")

            def expert_weights(n, half, static):
                pe.wait_ge(hot_ready, n + 1)
                if not static:
                    pe.wait_ge(w_read, n - 1)
                for q in range(4):
                    last = mm(ps[:, half, q * NE:(q + 1) * NE], hot[:, 4 * half + q, 0, :], hot[:, 4 * half + q, 1, :])
                last.then_inc(w_made, 1)

            for half in range(2):
                expert_weights(half, half, True)
            with pe.Fori(1, T // 8) as i:
                for half in range(2):
                    expert_weights(2 * i + half, half, False)
            s_made, s_read = flag("activations_made"), flag("activations_read")
            e_ready, e_added = flag("weighted_ready"), flag("experts_added")
            u_split, v_split = flag("u_split"), flag("v_split")
            pe.wait_ge(w_read, T // 4)
            pe.wait_ge(flag("h_split"), 1)

            def split_mm(out, high, low, rhs_high, rhs_low, first_, last_):
                mm(out, high, rhs_high, first_, False)
                mm(out, high, rhs_low, False, False)
                return mm(out, low, rhs_high, False, last_)

            def activations(c, q, static):
                pe.wait_ge(u_split, c + 1)
                if not (static and q < 2):
                    pe.wait_ge(s_read, c - 1)
                for k in range(KD):
                    e = slice(k * P, (k + 1) * P)
                    last = split_mm(ps[:, q % 2, 0:T], u_high[:, q % 2, e], u_low[:, q, e], h_high[:, k, :], h_low[:, k, :],
                                    k == 0, k == KD - 1)
                last.then_inc(s_made, 1)

            def add_experts(c, q, first_=False):
                pe.wait_ge(v_split, c + 1)
                pe.wait_ge(e_ready, c + 1)
                for m in range(KD):
                    e = slice(m * P, (m + 1) * P)
                    last = split_mm(sums[:, m, :], v_high[:, q % 2, e], v_low[:, q, e], w_high[q % 2], w_low[:, q % 2, :],
                                    first_ and m % 2 == 0, False)
                last.then_inc(e_added, 1)

            for q in range(4):
                activations(q, q, True)
                if q:
                    add_experts(q - 1, q - 1, q == 1)
            with pe.Fori(1, NE // 4) as i:
                for q in range(4):
                    activations(4 * i + q, q, False)
                    add_experts(4 * i + (q - 1), (q - 1) % 4)
            add_experts(NE - 1, 3)
            pe.wait_ge(flag("squares_ready"), 12)
            total("final_sum", [h[:, k, :] for k in range(KD)])

        @block.sync
        def _(sp):
            sp.dma_start(par[:, :], d["par"]).then_inc(loaded, 16)
            sp.dma_start(ssb, d["ssm_bc"]).then_inc(flag("ssm_bc_loaded"), 16)
            sp.dma_start(x[:, :, :], d["x"]).then_inc(flag("x_loaded"), 16)
            sp.dma_start(other, d["mem"]).then_inc(flag("mem_loaded"), 16)
            for n, (name, i, width) in enumerate(items):
                if (name, i) == ("xa_wo", 0):
                    sp.wait_ge(made, number(("xv", 1, 1)))
                    sp.dma_start(other, d["ctx"]).then_inc(flag("ctx_loaded"), 16)
                if n >= RING:
                    sp.wait_ge(made, released[n - RING])
                sp.dma_start(ring[:, n % RING, 0:width], d[name][i]).then_inc(in_ring[n % RING], 16)

            s_made, e_added = flag("activations_made"), flag("experts_added")
            for q in range(4):
                sp.wait_ge(made, emptied(q // 2))
                sp.dma_start(u_tile[:, q, :], d["peer_u"][q]).then_inc(flag(f"u_in{q}"), 16)
            for q in range(4):
                sp.wait_ge(made, emptied(2 + q // 2))
                sp.dma_start(v_tile[:, q, :], d["peer_v"][q]).then_inc(flag(f"v_in{q}"), 16)
            with sp.Fori(1, NE // 4) as i:
                for q in range(4):
                    sp.wait_ge(s_made, 4 * i + (q - 3))
                    sp.dma_start(u_tile[:, q, :], d["peer_u"][4 * i + q]).then_inc(flag(f"u_in{q}"), 16)
                    sp.wait_ge(e_added, 4 * i + (q - 3))
                    sp.dma_start(v_tile[:, q, :], d["peer_v"][4 * i + q]).then_inc(flag(f"v_in{q}"), 16)
            sp.wait_ge(flag("output_ready"), 1)
            sp.dma_start(d["out"], x).then_inc(flag("stored"), 16)
            sp.wait_ge(flag("stored"), 16)

        @block.vector
        def _(dve):
            v = nc.vector
            s = Steps(dve, "dve")
            link = s.link
            s_dt, s_a, s_th, s_k, s_mag, s_turn, s_co, s_si, s_ar, s_ai, s_fr, s_fi, s_den, s_t = (
                sm[:, i, :] for i in range(14))

            def rounded_off(out, f, tmp):
                link(v.tensor_scalar(tmp, f, MAGIC, None, ALU.add))
                link(v.tensor_scalar(tmp, tmp, MAGIC, None, ALU.subtract))
                link(v.tensor_tensor(out, f, tmp, ALU.subtract))

            def reciprocal_std(key, n=T, at=0):
                s.after(key, "act")
                r = std[:, at, 0:n]
                link(v.reciprocal(r, r))
                return r

            dve.wait_ge(loaded, 16)
            s.wait("ssm_dt_ready")
            link(v.tensor_tensor(s_a, cols("lam_re"), s_dt, ALU.mult))
            v.tensor_tensor(s_th, cols("lam_im"), s_dt, ALU.mult).then_inc(flag("ssm_a_ready"), 1)
            s.wait("ssm_a_ready")
            link(v.tensor_scalar(s_k, s_th, 0.15915494309, MAGIC, ALU.mult, ALU.add))
            link(v.tensor_scalar(s_k, s_k, MAGIC, None, ALU.subtract))
            for part in (PI_A, PI_B, PI_C):
                link(v.scalar_tensor_tensor(s_th, s_k, -part, s_th, ALU.mult, ALU.add))
            link(v.tensor_scalar(s_turn, s_th, 0.15915494309, None, ALU.mult))
            rounded_off(s_si, s_turn, s_t)
            link(v.tensor_scalar(s_co, s_turn, 0.25, None, ALU.add))
            rounded_off(s_co, s_co, s_t)
            v.memset(bb.rearrange("p i a c h -> p (i a c h)"), 0.0)
            v.memset(cc.rearrange("p i c h -> p (i c h)"), 0.0).then_inc(flag("turn_ready"), 1)
            s.wait("x_loaded", 16)
            r = reciprocal_std("mix_sum")
            for k in range(KD):
                last = v.scalar_tensor_tensor(h[:, k, :], x[:, k, :], col("mix_g", k), r, ALU.mult, ALU.mult)
            last.then_inc(flag("h_ready"), 1)
            bank = s.product("u")
            s.took("u", v.tensor_copy(u.rearrange("p a t -> p (a t)"), bank))
            s.wait("ssm_trig_ready", 2)
            link(v.tensor_tensor(s_ai, s_mag, s_si, ALU.mult))
            link(v.tensor_tensor(s_ar, s_mag, s_co, ALU.mult))
            link(v.tensor_scalar(s_ar, s_ar, 1.0, None, ALU.subtract))
            link(v.tensor_tensor(s_den, cols("lam_re"), cols("lam_re"), ALU.mult))
            link(v.tensor_tensor(s_t, cols("lam_im"), cols("lam_im"), ALU.mult))
            link(v.tensor_tensor(s_den, s_den, s_t, ALU.add))
            link(v.reciprocal(s_den, s_den))
            link(v.tensor_tensor(s_fr, s_ar, cols("lam_re"), ALU.mult))
            link(v.tensor_tensor(s_t, s_ai, cols("lam_im"), ALU.mult))
            link(v.tensor_tensor(s_fr, s_fr, s_t, ALU.add))
            link(v.tensor_tensor(s_fr, s_fr, s_den, ALU.mult))
            link(v.tensor_tensor(s_fi, s_ai, cols("lam_re"), ALU.mult))
            link(v.tensor_tensor(s_t, s_ar, cols("lam_im"), ALU.mult))
            link(v.tensor_tensor(s_fi, s_fi, s_t, ALU.subtract))
            link(v.tensor_tensor(s_fi, s_fi, s_den, ALU.mult))
            s.wait("ssm_bc_loaded", 16)
            fr = s_fr.unsqueeze(2).broadcast_to([P, NS, 16])
            fi = s_fi.unsqueeze(2).broadcast_to([P, NS, 16])
            b_re, b_im, c_re, c_im = (ssb[:, i] for i in range(4))
            link(v.tensor_tensor(bbt[:, 0], b_re, fr, ALU.mult))
            link(v.tensor_tensor(bbt[:, 1], b_im, fi, ALU.mult))
            link(v.tensor_tensor(bbt[:, 0], bbt[:, 0], bbt[:, 1], ALU.subtract))
            link(v.tensor_tensor(bbt[:, 1], b_im, fr, ALU.mult))
            link(v.tensor_tensor(b_im, b_re, fi, ALU.mult))
            link(v.tensor_tensor(bbt[:, 1], bbt[:, 1], b_im, ALU.add))
            for g in range(2):
                rows, at = slice(64 * g, 64 * g + 64), slice(16 * g, 16 * g + 16)
                for i in range(2):
                    src = bbt[rows, i, :, :]
                    dst = bb[rows, i, :, :, at].rearrange("p a c h -> p (a c) h")
                    v.tensor_copy(dst, src)
                v.tensor_copy(cc[rows, 0, :, at], c_re[rows])
                v.tensor_scalar(cc[rows, 1, :, at], c_re[rows], -1.0, None, ALU.mult)
                last = v.tensor_scalar(cc[rows, 2, :, at], c_im[rows], -1.0, None, ALU.mult)
            last.then_inc(flag("b_ready"), 1)
            link(v.memset(pad[:, :, 0:CW - 1], 0.0))
            s.after("conv_b", "act")
            bank = s.product("conv_a")
            s.took("conv_a", v.tensor_tensor(pad[:, :, CW - 1:], bank.rearrange("p (a t) -> p a t", a=2), glu_e, ALU.mult))
            for i in range(4):
                r = reciprocal_std(("qk_sum", i), 512, i % 2)
                g = col("sbq_g") if i < 2 else col("sbk_g")
                q2 = qk[:, 2 * i:2 * i + 2, :].rearrange("p a t -> p (a t)")
                ins = v.scalar_tensor_tensor(q2, q2, g, r, ALU.mult, ALU.mult)
                ins.then_inc(flag("qk_scaled"), 1)
            for c in range(NS):
                s.after(("bu", c), "act")
            s.wait("trig_ready", 2)
            co, si = trig[:, 0], trig[:, 1]
            link(v.tensor_tensor(rot[:, 0], co, bu[:, 0], ALU.mult))
            link(v.tensor_tensor(rot2, si, bu[:, 1], ALU.mult))
            link(v.tensor_tensor(rot[:, 0], rot[:, 0], rot2, ALU.add))
            link(v.tensor_tensor(rot[:, 1], co, bu[:, 1], ALU.mult))
            link(v.tensor_tensor(rot2, si, bu[:, 0], ALU.mult))
            link(v.tensor_tensor(rot[:, 1], rot[:, 1], rot2, ALU.subtract))
            for c in range(NS):
                for i in range(2):
                    last = v.tensor_tensor_scan(rot[:, i, c, :], s_mag[:, c:c + 1].to_broadcast([P, T]), rot[:, i, c, :],
                                                0.0, ALU.mult, ALU.add)
            link(last)
            link(v.tensor_tensor(bu[:, 0], co, rot[:, 0], ALU.mult))
            link(v.tensor_tensor(rot2, si, rot[:, 1], ALU.mult))
            link(v.tensor_tensor(bu[:, 0], bu[:, 0], rot2, ALU.subtract))
            link(v.tensor_tensor(bu[:, 1], si, rot[:, 0], ALU.mult))
            link(v.tensor_tensor(rot2, co, rot[:, 1], ALU.mult))
            v.tensor_tensor(bu[:, 1], bu[:, 1], rot2, ALU.add).then_inc(flag("states_ready"), 1)
            s.wait("states_ready")
            for j in range(CW):
                for a in range(2):
                    src, w = pad[:, a, j:j + T], col("dw_w", 2 * j + a)
                    if j == 0:
                        ins = v.tensor_scalar(conv[:, a, :], src, w, col("dw_b", a), ALU.mult, ALU.add)
                    else:
                        ins = v.scalar_tensor_tensor(conv[:, a, :], src, w, conv[:, a, :], ALU.mult, ALU.add)
                    ins.then_inc(flag("taps_done"), 1)
                    dve.wait_ge(flag("taps_done"), max(1, 2 * j + a))
            for g in range(6):
                bank = s.product(("mod", g))
                bias = cols("b_mod")[:, 8 * g:8 * g + 8].unsqueeze(2).broadcast_to([P, KD, 2])
                s.took(("mod", g), v.tensor_tensor(mod[:, g], bank[:, 0:16].rearrange("p (k c) -> p k c", c=2),
                                                        bias, ALU.add))
            s.after(("mod", 5))
            for i, (scale, which, g_) in enumerate(((1, 0, "norm1_g"), (1, 1, "norm1_g"), (4, 0, "norm2_g"))):
                v.scalar_tensor_tensor(gain[:, i, :], mod[:, scale, :, which], 1.0, cols(g_), ALU.add, ALU.mult)\
                    .then_inc(flag("gain_ready"), 1)
            bank = s.product("ssm_y")
            for a in range(2):
                last = v.scalar_tensor_tensor(ys[:, a, :], u[:, a, :], col("ssm_d", a), bank[:, a * T:(a + 1) * T],
                                              ALU.mult, ALU.add)
                if a == 0:
                    link(last)
            s.took("ssm_y", last)
            s.after("glu_b", "act")
            bank = s.product("glu_a")
            s.took("glu_a", v.tensor_tensor(ys.rearrange("p a t -> p (a t)"), bank, g_e.rearrange("p a t -> p (a t)"), ALU.mult))
            bank = s.product("ln_mean")
            s.wait("taps_done", 2 * CW)
            for a in range(2):
                last = v.scalar_tensor_tensor(conv[:, a, :], bank[:, 0:T], -1.0 / 256, conv[:, a, :], ALU.mult, ALU.add)
                if a == 0:
                    link(last)
            s.took("ln_mean", last)
            r = reciprocal_std("ln_var", T, 0)
            for a in range(2):
                link(v.tensor_tensor(conv[:, a, :], conv[:, a, :], r, ALU.mult))
                ins = v.tensor_scalar(conv[:, a, :], conv[:, a, :], col("ln_g", a), col("ln_b", a), ALU.mult, ALU.add)
                ins.then_inc(flag("ln_ready"), 1)
            bank = s.product("pw2")
            s.took("pw2", v.tensor_copy(cvo.rearrange("p a t -> p (a t)"), bank))

            def logits(hd):
                bank = s.product(("z", hd))
                s.took(("z", hd), v.tensor_scalar(z_s[:, hd % 2, :], bank[:, 0:384], SB_SCALE, None, ALU.mult))
                s.after(("z", hd))
                v.tensor_scalar(z_e[:, hd % 2, :], z_s[:, hd % 2, :], CLIP, None, ALU.min).then_inc(flag("z_clipped"), 1)

            def softplus(hd):
                s.wait("z_log_ready", hd + 1)
                v.tensor_tensor(z_p[:, hd % 2, :], z_s[:, hd % 2, :], z_e[:, hd % 2, :], ALU.max)\
                    .then_inc(flag("z_max_ready"), 1)

            def exponents(hd):
                bank = s.product(("later", hd))
                if hd >= 4:
                    dve.wait_ge(made, number(("o", (hd - 4) // 2)))
                s.took(("later", hd), v.tensor_tensor(z_w[:, hd % 4, :], z_s[:, hd % 2, :], bank[:, 0:384],
                                                           ALU.subtract))
                s.after(("later", hd))

            logits(0)
            logits(1)
            softplus(0)
            softplus(1)
            for hd in range(SB_H):
                exponents(hd)
                if hd + 2 < SB_H:
                    logits(hd + 2)
                if hd % 2 and hd + 2 < SB_H:
                    softplus(hd + 1)
                    softplus(hd + 2)
            s.after("ssm_sum", "act")
            s.after("glu_a")
            s.after("pw2")
            for key, at, src, n in (("ssm_sum", 0, ys, 2), ("conv_sum", 1, cvo, 2), ("sb_sum", 0, None, 4)):
                r = reciprocal_std(key, T, at)
                first_ = {"ssm_sum": 6, "conv_sum": 4, "sb_sum": 0}[key]
                for i in range(n):
                    dst = mixed[:, first_ + i, :]
                    last = v.scalar_tensor_tensor(dst, dst if src is None else src[:, i, :], col("branch_g", first_ + i), r,
                                                  ALU.mult, ALU.mult)
                last.then_inc(flag("mixed_ready"), 1)

            def add_to_x(key, i):
                bank = s.product((key, i))
                two = x[:, 2 * i:2 * i + 2, :].rearrange("p a t -> p (a t)")
                s.took((key, i), v.tensor_tensor(two, two, bank, ALU.add))

            for i in range(4):
                add_to_x("mix_out", i)
            def normed(key, src, dst, gain, at):
                r = reciprocal_std(key, T, at)
                for k in range(KD):
                    last = v.scalar_tensor_tensor(dst[:, k, :], src[:, k, :], col(gain, k), r, ALU.mult, ALU.mult)
                return last

            s.wait("mem_loaded", 16)
            normed("mem_sum", other, other, "mem_g", 0).then_inc(flag("other_ready"), 1)
            normed("xa_sum", x, h, "xa_g", 1).then_inc(flag("h_ready"), 1)
            for hd in range(XH):
                r = reciprocal_std(("xk_sum", hd), T, hd % 2)
                for j in range(2):
                    b = xk[:, 2 * hd + j, :]
                    last = v.scalar_tensor_tensor(b, b, col("xak_g", j), r, ALU.mult, ALU.mult)
                last.then_inc(flag("xk_scaled"), 1)
            for hd in range(XH):
                r = reciprocal_std(("xq_sum", hd), T, hd % 2)
                for j in range(2):
                    b = xq[:, 2 * hd + j, :]
                    last = v.scalar_tensor_tensor(b, b, col("xaq_g", j), r, ALU.mult, ALU.mult)
                last.then_inc(flag("xa_heads_ready"), 1)

            def top(hd):
                bank = s.product(("xs", hd)).rearrange("p (b t) -> p b t", b=2)
                s.took(("xs", hd), v.tensor_reduce(xs[:, hd, 0:2], bank, AX.X, ALU.max))
                s.after(("xs", hd), "dve")
                v.tensor_scalar(xs[:, hd, 2:4], xs[:, hd, 0:2], -1.0 / 16, None, ALU.mult).then_inc(flag("xa_max_ready"), 1)

            def shares(hd):
                s.after(("xs", hd), "act")
                link(v.reciprocal(xs[:, hd, 6:8], xs[:, hd, 4:6]))
                for b in range(TB):
                    last = v.tensor_scalar(xp[:, hd % 2, b, :], xp[:, hd % 2, b, :], xs[:, hd, 6 + b:7 + b], None, ALU.mult)
                last.then_inc(flag("xa_probs_ready"), 1)

            def outputs(hd):
                bank = s.product(("xo", hd))
                s.took(("xo", hd), v.tensor_copy(xo[:, 2 * hd:2 * hd + 2, :].rearrange("p a t -> p (a t)"), bank))

            top(0)
            for hd in range(XH):
                if hd + 1 < XH:
                    top(hd + 1)
                shares(hd)
                outputs(hd)
            for i in range(4):
                add_to_x("xa_out", i)
            def modulated(key, src, dst, which, at, g_, shift, done):
                r = reciprocal_std(key, T, at)
                for k in range(KD):
                    last = v.scalar_tensor_tensor(dst[:, k, :], src[:, k, :], gain[:, g_, k:k + 1], r, ALU.mult, ALU.mult)
                link(last)
                for k in range(KD):
                    last = v.tensor_scalar(dst[:, k, :], dst[:, k, :], mod[:, shift, k, which:which + 1], None, ALU.add)
                last.then_inc(flag(done), 1)

            normed("ffn_sum", x, h, "ffn_g", 0).then_inc(flag("h_ready"), 1)
            s.wait("gain_ready", 3)
            modulated("ctx_sum", other, other, 1, 1, 1, 0, "other_ready")
            for j in range(FB):
                s.after(("ffn", j), "act")
                bank = s.product(("ffn", j))
                s.took(("ffn", j), v.tensor_tensor(hid[:, j, :], bank[:, T:2 * T], f_e[:, j % 2, :], ALU.mult))
            dve.wait_ge(made, number(("ffn_out", FB // 2 - 1)))
            for i in range(4):
                two = x[:, 2 * i:2 * i + 2, :]
                last = v.tensor_tensor(two, two, sums[:, 2 * i:2 * i + 2, :], ALU.add)
                if i < 3:
                    link(last)
            s.took(("ffn_out", FB // 2 - 1), last)
            modulated("lat_sum", x, h, 0, 0, 0, 0, "h_ready")
            f_raw, f_log, f_sum, gd, run = (g_rows[:, i] for i in (1, 2, 5, 3, 4))
            bank = s.product("fg")
            s.took("fg", v.tensor_scalar(f_raw, bank[0:36, :], col("f_b", 0, 36), None, ALU.add))
            s.after("fg")
            v.tensor_scalar(f_log, f_raw, -CLIP, None, ALU.max).then_inc(flag("f_clipped"), 1)

            def short_conv(dst, src, c):
                w0, w1, w2 = (col("conv_w", 8 * j + c) for j in range(3))
                link(v.tensor_scalar(dst, src, w1, None, ALU.mult))
                spans = []
                if dst.shape[1] == 2 * T:
                    spans.append((dst[:, 1:T], src[:, 0:T - 1], dst[:, 0:T - 1], src[:, 1:T]))
                    dst, src = dst[:, T:2 * T], src[:, T:2 * T]
                d4, s4 = (t.rearrange("p (r n) -> p r n", n=64) for t in (dst, src))
                spans.append((d4[:, :, 1:], s4[:, :, :-1], d4[:, :, :-1], s4[:, :, 1:]))
                for d1, s1, _, _ in spans:
                    last = v.scalar_tensor_tensor(d1, s1, w0, d1, ALU.mult, ALU.add)
                link(last)
                for _, _, d1, s1 in spans:
                    last = v.scalar_tensor_tensor(d1, s1, w2, d1, ALU.mult, ALU.add)
                return last

            for c in range(MH):
                s.after(("mk", c), "act")
                last = short_conv(mk_t[:, c, :], mk_raw[:, c, :], 4 + c)
            last.then_inc(flag("conv2_ready"), 1)
            for c in range(MH):
                s.after(("mq", c // 2), "act")
                last = short_conv(mq_t[:, c, :], mq_raw[:, c, :], c)
            last.then_inc(flag("conv2_ready"), 1)
            for i in range(4):
                bank = s.product(("alpha", i))
                s.took(("alpha", i), v.tensor_scalar(la[:, i, :], bank, col("alpha_b", i), None, ALU.add))
            s.after(("alpha", 3))
            v.tensor_scalar(cs, la, -CLIP, None, ALU.max).then_inc(flag("alpha_clipped"), 1)
            s.wait("f_log_ready")
            link(v.scalar_tensor_tensor(f_raw, f_log, -1.0, f_raw, ALU.mult, ALU.min))
            fwd, bwd = slice(0, 32), slice(32, 36)
            one = lambda r: ones[r, 0:1].to_broadcast([r.stop - r.start, T])

            def running(dst, src, r, part, backwards, op, initial, by):
                lo, hi = part
                a, b = dst[r, lo:hi], src[r, lo:hi]
                if backwards:
                    a, b = a[:, ::-1], b[:, ::-1]
                return v.tensor_tensor_scan(a, one(r) if by is None else b, b, initial, *op)

            add_, max_ = (ALU.mult, ALU.add), (ALU.max, ALU.max)
            ctx_, lat_ = (0, T), (T, 2 * T)
            running(f_sum, f_raw, fwd, ctx_, True, add_, 0.0, None)
            running(f_sum, f_raw, fwd, lat_, False, add_, 0.0, None)
            running(f_sum, f_raw, bwd, ctx_, False, add_, 0.0, None)
            link(running(f_sum, f_raw, bwd, lat_, True, add_, 0.0, None))
            s.after("ig", "act")
            i_gate = g_rows[:, 0]
            link(v.tensor_tensor(gd[:, 0:T], i_gate[:, 0:T], f_raw[:, 0:T], ALU.subtract))
            link(v.tensor_tensor(gd[:, 0:T], gd[:, 0:T], f_sum[:, 0:T], ALU.add))
            v.tensor_tensor(gd[:, T:], i_gate[:, T:], f_sum[:, T:], ALU.subtract).then_inc(flag("gate_rows_ready"), 1)
            s.wait("gate_rows_ready")
            link(v.tensor_reduce(run[:, 0:1], gd[:, 0:T], AX.X, ALU.max))
            running(run, gd, fwd, lat_, False, max_, run[fwd, 0:1], 1)
            link(running(run, gd, bwd, lat_, True, max_, run[bwd, 0:1], 1))
            m_row = run[:, T:]
            link(v.tensor_tensor(m_row, m_row, f_sum[:, T:], ALU.add))
            link(v.tensor_scalar(m_row, m_row, 0.0, None, ALU.max))
            v.tensor_tensor(rows2[:, 0], f_sum[:, T:], m_row, ALU.subtract).then_inc(flag("m_rows_ready"), 1)
            s.wait("alpha_log_ready")
            link(v.scalar_tensor_tensor(la, cs, -1.0, la, ALU.mult, ALU.min))
            link(v.tensor_scalar(la, la, 1.0 / 16, None, ALU.mult))
            s.wait("reset_ready", 2)
            for i in range(4):
                a, b, r = cs[:, i, :], la[:, i, :], reset[:, i // 2, :]
                if i >= 2:
                    a, b, r = a[:, ::-1], b[:, ::-1], r[:, ::-1]
                last = v.tensor_tensor_scan(a, r, b, 0.0, ALU.mult, ALU.add)
            link(last)
            for dr in range(2):
                c4 = cs[:, 2 * dr:2 * dr + 2, :].rearrange("p i (c n) -> p (i c) n", n=GC)
                end = c4[:, :, 63:64] if dr == 0 else c4[:, :, 0:1]
                v.tensor_tensor(la[:, 2 * dr:2 * dr + 2, :].rearrange("p i (c n) -> p (i c) n", n=GC),
                                end.to_broadcast([P, 16, GC]), c4, ALU.subtract)
                for i in (2 * dr, 2 * dr + 1):
                    lat = cs[:, i, T:].rearrange("p (c n) -> p c n", n=GC)
                    mid = lat[:, :, 32 - dr:33 - dr]
                    last = v.tensor_tensor(q_in[:, i, :].rearrange("p (c n) -> p c n", n=GC), lat,
                                           mid.to_broadcast([P, 4, GC]), ALU.subtract)
            last.then_inc(flag("gla_diffs_ready"), 1)
            s.after(("gk", 1), "act")
            s.after("gq", "act")
            s.wait("gla_exps_ready", 4)
            for dr in range(2):
                at = slice(2 * dr, 2 * dr + 2)
                last = v.tensor_tensor(la[:, at, :], la[:, at, :], gk_t, ALU.mult)
            last.then_inc(flag("gla_ready"), 1)
            for dr in range(2):
                at = slice(2 * dr, 2 * dr + 2)
                v.tensor_tensor(k_in[:, at, :], k_in[:, at, :], gk_t[:, :, T:], ALU.mult)
                v.tensor_tensor(q_in[:, at, :], q_in[:, at, :], gq_t, ALU.mult)
                last = v.tensor_tensor(q_st[:, at, :], q_st[:, at, :], gq_t, ALU.mult)
            last.then_inc(flag("gla_ready"), 1)
            s.after("gcol", "act")

            def decays(hd):
                for dr in range(2):
                    bank = s.product(("row", hd, dr))
                    s.after(("row", hd, dr), "act")
                    r = 32 * dr + hd
                    for b in range(4):
                        last = v.tensor_scalar(dec[:, hd % 2, dr, b, :], bank[:, 0:T], gcol[:, b, r:r + 1], 0.0,
                                               ALU.add, ALU.min)
                    s.took(("row", hd, dr), last)

            def decayed(hd):
                e = dec[:, hd % 2]
                sc = P ** -0.5
                s.wait("decays_masked", 4 * (hd + 1))
                mul = lambda o, bk: v.scalar_tensor_tensor(o, bk, sc, o, ALU.mult, ALU.mult)
                bank = s.product(("ms", hd, 0)).rearrange("p (b t) -> p b t", b=2)
                mul(e[:, 0, 0:2, :], bank)
                s.took(("ms", hd, 0), mul(e[:, 1, 0:2, :], bank))
                bank = s.product(("ms", hd, 1)).rearrange("p (b t) -> p b t", b=2)
                mul(e[:, 0, 2, :], bank[:, 0, :])
                mul(e[:, 0, 3, P:T], bank[:, 1, P:T]).then_inc(flag("scores_ready"), 1)
                mul(e[:, 1, 2, 0:P], bank[:, 0, 0:P])
                s.took(("ms", hd, 1), mul(e[:, 1, 3, :], bank[:, 1, :]))

            def quotient(hd):
                for dr in range(2):
                    bank = s.product(("mn", hd, dr))
                    f = floor[:, hd % 2, dr, :]
                    link(v.scalar_tensor_tensor(f, bank[:, T:], -1.0, f, ALU.mult, ALU.max))
                    link(v.tensor_tensor(f, f, bank[:, T:], ALU.max))
                    link(v.reciprocal(f, f))
                    if dr == 0:
                        last = v.tensor_tensor(mlh[:, hd, :], bank[:, 0:T], f, ALU.mult)
                        s.took(("mn", hd, dr), last)
                        s.after(("mn", hd, dr))
                    else:
                        last = v.tensor_tensor(f, bank[:, 0:T], f, ALU.mult)
                        s.took(("mn", hd, dr), last)
                        s.after(("mn", hd, dr))
                        v.tensor_tensor(mlh[:, hd, :], mlh[:, hd, :], f, ALU.add).then_inc(flag("ml_heads_ready"), 1)

            decays(0)
            decayed(0)
            for hd in range(MH):
                if hd + 1 < MH:
                    decays(hd + 1)
                    decayed(hd + 1)
                quotient(hd)
            s.wait("q_zeroed", 2)
            for j in range(2):
                half = slice(64 * j, 64 * j + 64)
                last = v.tensor_copy(q_z[half, j], q_st[half])
            last.then_inc(flag("q_split"), 1)
            for i in range(4):
                dr = i // 2
                order = list(range(4)) if dr == 0 else [3, 2, 1, 0]
                bank = [s.product(("add", i, odd)).rearrange("p (b e) -> p b e", b=4) for odd in (0, 1)]
                add = lambda c: bank[c % 2][:, c // 2, :]
                run_s = st[:, i, 4, :]
                for n, c in enumerate(order):
                    dst = st[:, i, order[0], :] if n == 3 else run_s
                    if n == 0:
                        last = v.tensor_copy(dst, add(c))
                    else:
                        last = v.scalar_tensor_tensor(dst, run_s, e_end[:, i, c:c + 1], add(c), ALU.mult, ALU.add)
                    link(last)
                for n, c in enumerate(order[:3]):
                    last = v.scalar_tensor_tensor(st[:, i, order[n + 1], :], st[:, i, c, :], e_end[:, i, 4 + c:5 + c],
                                                  add(4 + c), ALU.mult, ALU.add)
                    if n == 0:
                        link(last)
                    else:
                        s.took(("add", i, c % 2), last)
                        s.after(("add", i, c % 2))
            for i in range(4):
                r = reciprocal_std(("mix2_sum", i), 512, i % 2)
                for j in range(2):
                    c = 2 * i + j
                    g_ = col("ml_g", c) if c < 4 else col("gla_g", c - 4)
                    last = v.scalar_tensor_tensor(mix2[:, c, :], mix2[:, c, :], g_, r[:, j * T:(j + 1) * T], ALU.mult, ALU.mult)
                link(last)
                s.after(("mo", i) if i < 2 else ("gr", i - 2), "act")
                two = slice(2 * i, 2 * i + 2)
                v.tensor_tensor(mix2[:, two, :], mix2[:, two, :], out_g[:, two, :], ALU.mult).then_inc(flag("mix2_ready"), 1)
            for i in range(4):
                bank = s.product(("mix2_out", i))
                for j in range(2):
                    k = 2 * i + j
                    last = v.scalar_tensor_tensor(x[:, k, :], bank[:, j * T:(j + 1) * T], mod[:, 2, k, 0:1], x[:, k, :],
                                                  ALU.mult, ALU.add)
                s.took(("mix2_out", i), last)
            modulated("peer_sum", x, h, 0, 0, 2, 3, "h_ready")
            NONE = -3.0e38

            def top16(values, indices, src, rest):
                link(v.max(values[:, 0:8], src))
                v.max_index(indices[:, 0:8], values[:, 0:8], src)
                link(v.match_replace(rest, values[:, 0:8], src, NONE))
                link(v.max(values[:, 8:16], rest))
                return v.max_index(indices[:, 8:16], values[:, 8:16], rest)

            for b in range(TB):
                for j in range(2 * PH):
                    s.after(("psc", b, j // 4), "act")
                    last = top16(tv[:, b, j // 2, j % 2, :], ti[:, b, j // 2, j % 2, :], psc[:, b, j, :], psc2[:, j % 2, :])
                link(last)
                link(v.tensor_copy(tf[:, b], ti[:, b]))
                four = [P, PH, TOPK, TOPK]
                link(v.tensor_tensor(cand, tv[:, b, :, 0, :].unsqueeze(3).broadcast_to(four),
                                     tv[:, b, :, 1, :].unsqueeze(2).broadcast_to(four), ALU.add))
                for j in range(PH):
                    last = top16(bv[:, b, j, :], bi[:, b, j, :], cand[:, j].rearrange("p a c -> p (a c)"), cand2)
                link(last)
                w3 = keys3[:, 2, b]
                v.tensor_tensor(w3, bv[:, b], bv[:, b, :, 0:1].to_broadcast([P, PH, TOPK]), ALU.subtract)\
                    .then_inc(flag("best_ready"), 1)
                v.tensor_scalar(side[:, 0, b], bi[:, b], 4, None, ALU.logical_shift_right)
                link(v.tensor_scalar(side[:, 1, b], bi[:, b], 15, None, ALU.bitwise_and))
                for i in range(2):
                    last = v.tensor_copy(side_f[:, i, b], side[:, i, b])
                link(last)
                sixteen = iota[:, 0:TOPK].unsqueeze(1).unsqueeze(1).broadcast_to(four)
                for i in range(2):
                    link(v.tensor_tensor(hit, side_f[:, i, b].unsqueeze(3).broadcast_to(four), sixteen, ALU.is_equal))
                    link(v.tensor_tensor(hit, hit, tf[:, b, :, i, :].unsqueeze(2).broadcast_to(four), ALU.mult))
                    link(v.tensor_reduce(keys3[:, i, b], hit, AX.X, ALU.add))
                s.wait("best_exp_ready", b + 1)
                link(v.tensor_reduce(bsum[:, b], w3, AX.X, ALU.add))
                link(v.reciprocal(bsum[:, b], bsum[:, b]))
                v.tensor_tensor(w3, w3, bsum[:, b].unsqueeze(2).broadcast_to([P, PH, TOPK]), ALU.mult)\
                    .then_inc(flag("picked"), 1)
            s.after(("keys3", 0), "act")
            s.after(("keys3", 1), "act")
            s.wait("h_high_ready")
            dve.wait_ge(made, number(("pq", PH - 1)))
            v.tensor_tensor(h_low, h, h_high.bitcast(F32), ALU.subtract).then_inc(flag("h_split"), 1)
            dve.wait_ge(made, emptied(RING - 2))
            hot_ready, w_made = flag("one_hot_ready"), flag("expert_weights_made")

            def one_hot(t, half):
                for q in range(4):
                    at = t + q
                    k1, wt = (idx[:, i, bass.ds(at, 1)] for i in (0, 2))
                    v.tensor_scalar(hot[:, 4 * half + q, 0, :], iota, k1, wt, ALU.is_equal, ALU.mult)
                last = v.tensor_tensor(hot[:, 4 * half:4 * half + 4, 1, :], iota.unsqueeze(1).broadcast_to([P, 4, NE]),
                                       idx[:, 1, bass.ds(t, 4)].unsqueeze(2).broadcast_to([P, 4, NE]), ALU.is_equal)
                last.then_inc(hot_ready, 1)

            for half in range(2):
                one_hot(4 * half, half)
            with dve.Fori(1, T // 8) as i:
                for half in range(2):
                    dve.wait_ge(w_made, 2 * i + (half - 1))
                    one_hot(8 * i + 4 * half, half)
            s_read, e_ready, e_added = flag("activations_read"), flag("weighted_ready"), flag("experts_added")

            def low_of(kind, c, q):
                tile, high, low = (u_tile, u_high, u_low) if kind == "u" else (v_tile, v_high, v_low)
                dve.wait_ge(flag(kind + "_high_ready"), c + 1)
                v.tensor_tensor(low[:, q, :], tile[:, q, :], high[:, q % 2, :].bitcast(F32), ALU.subtract)\
                    .then_inc(flag(kind + "_split"), 1)

            def weighted(c, q, static):
                a, g_ = act_e[:, q % 2, :], g_all[:, :, bass.ds(c, 1)].rearrange("p t o -> p (t o)")
                dve.wait_ge(s_read, c + 1)
                if not (static and q < 2):
                    dve.wait_ge(e_added, c - 1)
                v.tensor_tensor(w_high[q % 2], a, g_, ALU.mult)
                v.tensor_tensor(a, a, g_, ALU.mult).then_inc(flag("whole_weighted"), 1)
                dve.wait_ge(flag("whole_weighted"), c + 1)
                v.tensor_tensor(w_low[:, q % 2, :], a, w_high[q % 2].bitcast(F32), ALU.subtract).then_inc(e_ready, 1)

            def experts(i, static, last_=False):
                for q in range(4):
                    c = 4 * i + q
                    weighted(c, q, static)
                    if not (last_ and q >= 2):
                        low_of("u", c + 2, (q + 2) % 4)
                    if not (last_ and q >= 3):
                        low_of("v", c + 1, (q + 1) % 4)

            low_of("u", 0, 0)
            low_of("u", 1, 1)
            low_of("v", 0, 0)
            dve.wait_ge(flag("expert_weights_read"), T // 4)
            experts(0, True)
            with dve.Fori(1, NE // 4 - 1) as i:
                experts(i, False)
            experts(NE // 4 - 1, False, True)
            dve.wait_ge(e_added, NE)
            for k in range(KD):
                last = v.scalar_tensor_tensor(x[:, k, :], sums[:, k, :], mod[:, 5, k, 0:1], x[:, k, :], ALU.mult, ALU.add)
            last.then_inc(flag("x_final"), 1)
            s.after("final_sum", "act")
            r = std_f
            link(v.reciprocal(r, r))
            for k in range(KD):
                last = v.scalar_tensor_tensor(x[:, k, :], x[:, k, :], col("normf_g", k), r, ALU.mult, ALU.mult)
            last.then_inc(flag("output_ready"), 1)

        @block.scalar
        def _(act):
            a_ = nc.scalar.activation
            s = Steps(act, "act")

            def squares(dst, src):
                return a_(dst, src, ACT.Square)

            def std_of(key, count, n=T, at=0):
                bank = s.product(key)
                s.took(key, a_(std[:, at, 0:n], bank[:, 0:n], ACT.Sqrt, bias=eps[:, :], scale=1.0 / count))

            def copy_out(key, dst, src=None, scale=1.0):
                bank = s.product(key)
                s.took(key, a_(dst, bank if src is None else src(bank), ACT.Copy, scale=scale))

            def halves(bank):
                return bank.rearrange("p (a t) -> p a t", a=2)

            act.wait_ge(loaded, 16)
            a_(sm[:, 0, :], cols("log_dt"), ACT.Exp).then_inc(flag("ssm_dt_ready"), 1)
            s.wait("ssm_a_ready")
            a_(sm[:, 4, :], sm[:, 1, :], ACT.Exp).then_inc(flag("mag_ready"), 1)
            s.wait("x_loaded", 16)
            squares(sq, x[:, :, :]).then_inc(flag("squares_ready"), 1)
            s.wait("turn_ready")
            for i in (6, 7):
                a_(sm[:, i, :], sm[:, i, :], ACT.Sin, scale=TURN).then_inc(flag("ssm_trig_ready"), 1)
            s.wait("constants_ready", 5)
            std_of("mix_sum", D)
            bank = s.product("conv_b")
            s.took("conv_b", a_(glu_e, halves(bank), ACT.Sigmoid))
            a_(cond[:, :, 0], cols("c"), ACT.Silu)
            a_(cond[:, :, 1], cols("c_ctx"), ACT.Silu).then_inc(flag("cond_ready"), 1)
            for b in range(TB):
                copy_out(("v", b), v_sb[:, b, :])
            for i in range(4):
                bank = s.product(("qk", i))
                a_(qk[:, 2 * i:2 * i + 2, :], halves(bank), ACT.Copy)
                s.took(("qk", i), squares(sq[:, 2 * i:2 * i + 2, :], halves(bank)))
            copy_out("b_t", bb_t.rearrange("p i a s -> p (i a s)"))
            for c in range(NS):
                copy_out(("bu", c), bu[:, :, c, :], halves)
            s.wait("turns_ready", 2)
            for i in range(2):
                t = trig[:, i].rearrange("p c t -> p (c t)")
                a_(t, t, ACT.Sin, scale=TURN).then_inc(flag("trig_ready"), 1)
            s.after(("qk", 3), "act")
            a_(sm[:, 21, 0:1], sm[:, 0, 0:1], ACT.Copy).then_inc(flag("squares_ready"), 1)
            s.wait("h_ready")
            for i in range(4):
                if i >= 2:
                    s.wait("qk_scaled", i - 1)
                std_of(("qk_sum", i), SB_D, 512, i % 2)
            bank = s.product("glu_b")
            s.took("glu_b", a_(g_e, halves(bank), ACT.Sigmoid))
            s.after("glu_a", "dve")
            squares(sq[:, 6:8, :], ys).then_inc(flag("branch_squares_ready"), 1)
            s.after("ln_mean", "dve")
            squares(glu_e, conv).then_inc(flag("conv_squares_ready"), 1)
            s.wait("qk_scaled", 4)
            std_of("ln_var", 256)
            s.wait("ln_ready", 2)
            a_(conv, conv, ACT.Silu).then_inc(flag("conv_ready"), 1)
            s.after("pw2", "dve")
            squares(sq[:, 4:6, :], cvo).then_inc(flag("branch_squares_ready"), 1)

            def log1p_exp(hd):
                s.wait("z_clipped", hd + 1)
                z = z_e[:, hd % 2, :]
                s.link(a_(z, z, ACT.Exp))
                a_(z, z, ACT.Ln, bias=1.0).then_inc(flag("z_log_ready"), 1)

            def exp_weights(hd):
                s.wait("exponents_masked", 2 * (hd + 1))
                w = z_w[:, hd % 4, :]
                a_(w, w, ACT.Exp).then_inc(flag("sb_weights_ready"), 1)

            def heads_out(pair):
                bank = s.product(("o", pair))
                a_(mixed[:, pair, :], bank[:, 0:T], ACT.Copy)
                s.took(("o", pair), squares(sq[:, pair, :], bank[:, 0:T]))

            log1p_exp(0)
            log1p_exp(1)
            for hd in range(SB_H):
                exp_weights(hd)
                if hd + 2 < SB_H:
                    log1p_exp(hd + 2)
                if hd % 2 and hd > 1:
                    heads_out(hd // 2 - 1)
            heads_out(SB_H // 2 - 1)
            s.after(("o", SB_H // 2 - 1), "act")
            a_(sm[:, 21, 0:1], sm[:, 0, 0:1], ACT.Copy).then_inc(flag("branch_squares_ready"), 1)
            std_of("ssm_sum", 256, T, 0)
            std_of("conv_sum", 256, T, 1)
            s.wait("mixed_ready", 1)
            std_of("sb_sum", 512, T, 0)
            s.wait("mem_loaded", 16)
            squares(sq, other).then_inc(flag("squares_ready"), 1)
            s.wait("mixed_ready", 3)
            std_of("mem_sum", D, T, 0)
            s.after(("mix_out", 3), "dve")
            squares(sq, x[:, :, :]).then_inc(flag("squares_ready"), 1)
            std_of("xa_sum", D, T, 1)

            def heads_raw(key, i, dst):
                bank = s.product((key, i))
                a_(dst[:, 2 * i:2 * i + 2, :], halves(bank), ACT.Copy)
                s.took((key, i), squares(sq[:, 2 * i:2 * i + 2, :], halves(bank)))

            for i in range(4):
                heads_raw("xk", i, xk)
            s.after(("xk", 3), "act")
            a_(xs[:, 0, 0:1], eps[:, :], ACT.Copy).then_inc(flag("squares_ready"), 1)
            for n in range(2):
                for b in range(TB):
                    copy_out(("xv", n, b), xv[:, b, 512 * n:512 * n + 512])
            s.wait("h_ready", 2)
            for hd in range(XH):
                if hd >= 2:
                    s.wait("xk_scaled", hd - 1)
                std_of(("xk_sum", hd), XD, T, hd % 2)
            for i in range(4):
                heads_raw("xq", i, xq)
            s.after(("xq", 3), "act")
            a_(xs[:, 0, 0:1], eps[:, :], ACT.Copy).then_inc(flag("squares_ready"), 1)
            s.wait("xk_scaled", 4)
            for hd in range(XH):
                if hd >= 2:
                    s.wait("xa_heads_ready", hd - 1)
                std_of(("xq_sum", hd), XD, T, hd % 2)

            def exps(hd):
                s.wait("xa_max_ready", hd + 1)
                if hd >= 2:
                    act.wait_ge(made, number(("xpt", hd - 2)))
                bank = s.product(("xs", hd))
                for b in range(TB):
                    last = a_(xp[:, hd % 2, b, :], bank[:, b * T:(b + 1) * T], ACT.Exp, bias=xs[:, hd, 2 + b:3 + b],
                              scale=1.0 / 16, accum_out=xs[:, hd, 4 + b:5 + b])
                s.took(("xs", hd), last)

            exps(0)
            for hd in range(XH):
                if hd + 1 < XH:
                    exps(hd + 1)
                if hd >= 2:
                    act.wait_ge(made, number(("xo", hd - 2)))
                copy_out(("xpt", hd), xpt[:, hd % 2, :, :], halves)
            s.after(("xa_out", 3), "dve")
            squares(sq, x[:, :, :]).then_inc(flag("squares_ready"), 1)
            std_of("ffn_sum", D, T, 0)
            s.wait("ctx_loaded", 16)
            squares(sq, other).then_inc(flag("squares_ready"), 1)
            std_of("ctx_sum", D, T, 1)
            for j in range(FB):
                if j >= 2:
                    s.after(("ffn", j - 2), "dve")
                bank = s.product(("ffn", j))
                s.took(("ffn", j), a_(f_e[:, j % 2, :], bank[:, 0:T], ACT.Silu))
            act.wait_ge(made, number("ctx_sum"))
            s.after(("ffn_out", FB // 2 - 1), "dve")
            act.dma_start(lr_w, d["lr_w"]).then_inc(flag("lr_loaded"), 16)
            squares(sq, x[:, :, :]).then_inc(flag("squares_ready"), 1)
            std_of("lat_sum", D, T, 0)
            bank = s.product("ig")
            s.took("ig", a_(g_rows[:, 0], bank[0:36, :], ACT.Identity, bias=col("ig_b", 0, 36)))
            copy_out("glr", glr, lambda b: b[0:32, :])
            for c in range(MH):
                copy_out(("mk", c), mk_raw[:, c, :])
            for c in range(2):
                copy_out(("gk", c), gk_t[:, c, :])
            for i in range(2):
                copy_out(("mq", i), mq_raw[:, 2 * i:2 * i + 2, :], halves)
            copy_out("gq", gq_t, halves, scale=GC ** -0.5)
            s.wait("f_clipped")
            s.link(a_(g_rows[:, 2], g_rows[:, 2], ACT.Exp, scale=-1.0))
            a_(g_rows[:, 2], g_rows[:, 2], ACT.Ln, bias=1.0).then_inc(flag("f_log_ready"), 1)
            for b in range(4):
                copy_out(("mv", b), mv[:, b, :])
            s.wait("alpha_clipped")
            s.link(a_(cs, cs, ACT.Exp, scale=-1.0))
            a_(cs, cs, ACT.Ln, bias=1.0).then_inc(flag("alpha_log_ready"), 1)
            s.wait("conv2_ready", 2)
            a_(mk_t, mk_t, ACT.Silu).then_inc(flag("mkq_ready"), 1)
            a_(mq_t, mq_t, ACT.Silu).then_inc(flag("mkq_ready"), 1)
            for b in range(4):
                copy_out(("gv", b), gv[:, b, :])
            s.wait("m_rows_ready")
            a_(rows2[:, 1], g_rows[:, 4, T:], ACT.Exp, scale=-1.0).then_inc(flag("m_rows_ready"), 1)
            copy_out("gcol", gcol.rearrange("p b r -> p (b r)"), lambda b: b[:, 0:4 * 36])
            s.wait("gla_diffs_ready")
            done = flag("gla_exps_ready")
            a_(k_in, q_in, ACT.Exp, scale=-1.0)
            a_(q_st, cs[:, :, T:], ACT.Exp).then_inc(done, 1)
            a_(q_in, q_in, ACT.Exp).then_inc(done, 1)
            a_(la, la, ACT.Exp).then_inc(done, 1)
            ends = cs.rearrange("p (d i) (c n) -> p d i c n", d=2, n=GC)
            for dr in range(2):
                last = a_(e_end[:, 2 * dr:2 * dr + 2, :], ends[:, dr, :, :, 63 if dr == 0 else 0], ACT.Exp)
            last.then_inc(done, 1)

            def exps_of_decays(hd):
                for dr in range(2):
                    bank = s.product(("row", hd, dr))
                    if hd >= 2:
                        s.after(("mn", hd - 2, dr), "dve")
                    s.took(("row", hd, dr), a_(floor[:, hd % 2, dr, :], bank[:, T:], ACT.Copy))
                    s.after(("row", hd, dr), "dve")
                    e = dec[:, hd % 2, dr]
                    a_(e, e, ACT.Exp).then_inc(flag("decays_ready"), 1)

            for hd in range(MH):
                exps_of_decays(hd)
            for i in range(4):
                copy_out(("kd", i), kd_t[:, i, :, :].rearrange("p b c -> p (b c)"))
            s.wait("att_zeroed")
            for j in range(2):
                bank = s.product(("att", j))
                for odd in range(2):
                    r = slice(64 * odd, 64 * odd + 64)
                    n = bank[r].rearrange("p (m t) -> p m t", t=GC)
                    dst = att[r, j].rearrange("p d b h t -> p (d b h) t")[:, :, odd * GC:(odd + 1) * GC]
                    last = a_(dst, n, ACT.Copy)
                s.took(("att", j), last)
            for pair in range(2):
                copy_out(("go", pair), glh[:, 2 * pair:2 * pair + 2, :], halves)
            s.after(("go", 1), "act")
            s.wait("ml_heads_ready", MH)
            squares(dec_sq, mix2).then_inc(flag("squares_ready"), 1)
            for i in range(2):
                bank = s.product(("mo", i))
                s.took(("mo", i), a_(out_g[:, 2 * i:2 * i + 2, :], halves(bank), ACT.Sigmoid))
            for i in range(2):
                bank = s.product(("gr", i))
                s.took(("gr", i), a_(out_g[:, 4 + 2 * i:6 + 2 * i, :], halves(bank), ACT.Silu))
            for i in range(4):
                if i >= 2:
                    s.wait("mix2_ready", i - 1)
                std_of(("mix2_sum", i), P, 512, i % 2)
            s.after(("mix2_out", 3), "dve")
            squares(sq, x[:, :, :]).then_inc(flag("squares_ready"), 1)
            std_of("peer_sum", D, T, 0)
            s.wait("h_ready", 5)
            a_(h_high, h[:, :, :], ACT.Copy).then_inc(flag("h_high_ready"), 1)
            for i in range(PH):
                copy_out(("pq", i), pq[:, 2 * i:2 * i + 2, :], halves)
            for b in range(TB):
                for g in range(4):
                    copy_out(("psc", b, g), psc[:, b, 4 * g:4 * g + 4, :].rearrange("p j e -> p (j e)"))
            for b in range(TB):
                s.wait("best_ready", b + 1)
                w3 = keys3[:, 2, b]
                a_(w3, w3, ACT.Exp).then_inc(flag("best_exp_ready"), 1)
                copy_out(("keys3", b), idx[:, :, b * P:(b + 1) * P], lambda bk: bk[:, 0:3 * P].rearrange("p (i t) -> p i t", i=3))
            w_made, w_read = flag("expert_weights_made"), flag("expert_weights_read")

            def keep_weights(t, n, half):
                act.wait_ge(w_made, n + 1)
                a_(g_all[:, bass.ds(t, 4), :], ps[:, half, :].rearrange("p (t e) -> p t e", e=NE), ACT.Copy).then_inc(w_read, 1)

            with act.Fori(0, T // 8) as i:
                for half in range(2):
                    keep_weights(8 * i + 4 * half, 2 * i + half, half)
            s_made, s_read, e_ready = flag("activations_made"), flag("activations_read"), flag("weighted_ready")
            e_added = flag("experts_added")
            act.wait_ge(w_made, T // 4)

            def high_of(kind, i, c, q, static):
                tile, high, used = (u_tile, u_high, s_made) if kind == "u" else (v_tile, v_high, e_added)
                act.wait_ge(flag(f"{kind}_in{q % 4}"), 16 * i + 16 * (q // 4 + 1))
                if not (static and q < 2):
                    act.wait_ge(used, c - 1)
                a_(high[:, q % 2, :], tile[:, q % 4, :], ACT.Copy).then_inc(flag(kind + "_high_ready"), 1)

            def activate(i, static, last_=False):
                for q in range(4):
                    c = 4 * i + q
                    act.wait_ge(s_made, c + 1)
                    if not (static and q < 2):
                        act.wait_ge(e_added, c - 1)
                    a_(act_e[:, q % 2, :], ps[:, q % 2, 0:T], ACT.Gelu).then_inc(s_read, 1)
                    if not (last_ and q >= 2):
                        high_of("u", i, c + 2, q + 2, static)
                    if not (last_ and q >= 3):
                        high_of("v", i, c + 1, q + 1, static)

            high_of("u", 0, 0, 0, True)
            high_of("u", 0, 1, 1, True)
            high_of("v", 0, 0, 0, True)
            activate(0, True)
            with act.Fori(1, NE // 4 - 1) as i:
                activate(i, False)
            activate(NE // 4 - 1, False, True)
            s.wait("x_final")
            squares(h, x[:, :, :]).then_inc(flag("squares_ready"), 1)
            bank = s.product("final_sum")
            s.took("final_sum", a_(std_f, bank[:, 0:T], ACT.Sqrt, bias=eps[:, :], scale=1.0 / D))

        @block.gpsimd
        def _(pool):
            g = nc.gpsimd
            s = Steps(pool, "pool")
            link = s.link
            ready = flag("constants_ready")
            g.memset(eps[:, :], EPS)
            g.memset(ones[:, :], 1.0).then_inc(ready, 1)
            link(g.memset(pair1, 0.0))
            g.iota(iota[:, :], pattern=[[1, P]], base=0, channel_multiplier=0, allow_small_or_imprecise_dtypes=True)\
                .then_inc(ready, 1)
            link(g.iota(ramp, pattern=[[1, T]], base=0, channel_multiplier=0, allow_small_or_imprecise_dtypes=True))
            link(g.memset(pair1[0:64, 0:64], 1.0))
            g.memset(pair1[64:P, 64:P], 1.0).then_inc(ready, 1)
            s.wait("constants_ready", 3)
            link(g.memset(ident[:, :], 0.0))
            g.affine_select(ident[:, :], ident[:, :], pattern=[[-1, P]], compare_op=ALU.not_equal, fill=1.0, base=0,
                            channel_multiplier=1).then_inc(ready, 1)
            link(g.memset(lower, 1.0))
            g.affine_select(lower, lower, pattern=[[-1, P]], compare_op=ALU.is_ge, fill=0.0, base=0,
                            channel_multiplier=1).then_inc(ready, 1)
            s.wait("turn_ready")
            for c in range(NS):
                last = g.tensor_scalar(trig[:, 1, c, :], ramp, sm[:, 5, c:c + 1], None, ALU.mult)
            link(last)
            link(g.tensor_scalar(trig[:, 0], trig[:, 1], 0.25, None, ALU.add))
            for i in range(2):
                link(g.tensor_scalar(rot[:, i], trig[:, i], MAGIC, None, ALU.add))
                link(g.tensor_scalar(rot[:, i], rot[:, i], MAGIC, None, ALU.subtract))
                g.tensor_tensor(trig[:, i], trig[:, i], rot[:, i], ALU.subtract).then_inc(flag("turns_ready"), 1)

            def before_query(tile, name, fill=0.0):
                for at in (0, T):
                    t = tile[:, at:at + P]
                    g.affine_select(t, t, pattern=[[1, P]], compare_op=ALU.is_gt, fill=fill, base=0,
                                    channel_multiplier=-1).then_inc(flag(name), 1)

            def mask_softplus(hd):
                s.wait("z_max_ready", hd + 1)
                before_query(z_p[:, hd % 2, :], "softplus_ready")

            mask_softplus(0)
            mask_softplus(1)
            for hd in range(SB_H):
                s.after(("later", hd), "dve")
                before_query(z_w[:, hd % 4, :], "exponents_masked", NEVER)
                if hd + 2 < SB_H:
                    mask_softplus(hd + 2)
            s.after(("ffn_out", FB // 2 - 1), "dve")
            link(g.memset(reset, 1.0))
            chunks = reset.rearrange("p d (c n) -> p d c n", n=GC)
            g.memset(chunks[:, 0, :, 0], 0.0).then_inc(flag("reset_ready"), 1)
            g.memset(chunks[:, 1, :, GC - 1], 0.0).then_inc(flag("reset_ready"), 1)

            def seen(t, sign, base, n, name):
                g.affine_select(t, t, pattern=[[sign, n]], compare_op=ALU.is_ge, fill=0.0, base=base,
                                channel_multiplier=-sign).then_inc(flag(name), 1)

            for hd in range(MH):
                e = dec[:, hd % 2]
                s.wait("decays_ready", 2 * hd + 1)
                seen(e[:, 0, 2, :], 1, 0, T, "decays_masked")
                seen(e[:, 0, 3, P:T], 1, 0, P, "decays_masked")
                s.wait("decays_ready", 2 * hd + 2)
                seen(e[:, 1, 2, 0:P], -1, 0, P, "decays_masked")
                seen(e[:, 1, 3, :], -1, P, T, "decays_masked")
            pool.wait_ge(made, number(("mn", MH - 1, 1)))
            g.memset(att, 0.0).then_inc(flag("att_zeroed"), 1)
            s.wait("att_zeroed")
            g.memset(q_z[64:P, 0], 0.0).then_inc(flag("q_zeroed"), 1)
            s.wait("q_zeroed", 1)
            g.memset(q_z[0:64, 1], 0.0).then_inc(flag("q_zeroed"), 1)
            s.wait("q_zeroed", 2)
            for j in range(2):
                s.after(("att", j), "act")
                for dr in range(2):
                    t = att[:, j, dr].rearrange("p b h t -> p (b h) t")
                    sign = 1 - 2 * dr
                    g.affine_select(t, t, pattern=[[0, 4], [sign, P]], compare_op=ALU.is_ge, fill=0.0, base=0,
                                    channel_multiplier=-sign).then_inc(flag("att_ready"), 1)


def blocks(w):
    k, n = w.shape
    return w.reshape(k // P, P, n // 256, 2, P).transpose(2, 1, 3, 0, 4).reshape(n // 256, P, -1)


def rows(w, k):
    kk, n = w.shape
    return w.reshape(kk // (P * k), k, P, n).transpose(0, 2, 1, 3).reshape(-1, P, k * n)


def features(a):
    t, f = a.shape
    return a.T.reshape(f // P, P, t).transpose(1, 0, 2)


def lay_out(i):
    import numpy as np
    o = {}
    vec = lambda a: a.reshape(-1, P).T
    states = lambda a: a.reshape(NS, P).T
    two = lambda a: np.concatenate([a, a]).reshape(P, 1)

    def gate_bias(a, kind):
        out = np.zeros((P, 1), np.float32)
        for dr in range(2):
            out[32 * dr:32 * dr + MH, 0] = a.reshape(2, 2, MH)[dr, kind]
        return out

    taps = i["conv_dw_w"][0]
    short = i["ml_conv_w_2"][0]
    p = {
        "mix_g": vec(i["norm_mix_g"][0]), "sbq_g": two(i["sb_q_norm_g"][0]), "sbk_g": two(i["sb_k_norm_g"][0]),
        "dw_w": taps.reshape(CW * 2, P).T, "dw_b": vec(i["conv_dw_b"][0]), "ln_g": vec(i["conv_ln_g"][0]),
        "ln_b": vec(i["conv_ln_b"][0]), "lam_re": states(i["ssm_lam_re"][0]), "lam_im": states(i["ssm_lam_im"][0]),
        "log_dt": states(np.repeat(i["ssm_log_dt"][0], 64)), "ssm_d": vec(i["ssm_d"][0]),
        "branch_g": vec(i["branch_norm_g"][0]), "xa_g": vec(i["norm_xa_g"][0]), "mem_g": vec(i["norm_mem_g"][0]),
        "xaq_g": vec(i["xa_q_norm_g"][0]), "xak_g": vec(i["xa_k_norm_g"][0]), "ffn_g": vec(i["norm_ffn_g"][0]),
        "c": vec(i["c_2"][0]), "c_ctx": vec(i["c_ctx_2"]), "b_mod": vec(i["b_mod_2"][0]),
        "norm1_g": vec(i["norm1_g_2"][0]), "conv_w": short.reshape(24, P).T,
        "ig_b": gate_bias(i["ml_gate_b_2"][0], 0), "f_b": gate_bias(i["ml_gate_b_2"][0], 1),
        "ml_g": vec(i["ml_norm_g_2"][0]), "alpha_b": i["gla_alpha_b_2"][0].reshape(4, P).T,
        "gla_g": vec(i["gla_norm_g_2"][0]), "norm2_g": vec(i["norm2_g_2"][0]), "normf_g": vec(i["norm_f_g_2"]),
    }
    o["par"] = np.concatenate([p[n] for n in COLS], axis=1)
    o["x"], o["mem"], o["ctx"] = features(i["x"][0]), features(i["mem"][0]), features(i["ctx_2"][0])
    by_state = lambda a: a.reshape(NS, P, 16).transpose(1, 0, 2)
    o["ssm_bc"] = np.stack([by_state(i["ssm_b_re"][0]), by_state(i["ssm_b_im"][0]),
                            by_state(i["ssm_c_re"][0].transpose(0, 2, 1)), by_state(i["ssm_c_im"][0].transpose(0, 2, 1))], axis=1)
    w = i["w_in"][0]
    o["w_in"], o["w_in_v"] = blocks(w), rows(w[:, 1024:1536], 4)
    o["w_mod"] = blocks(i["w_mod_2"][0])
    o["ssm_glu"] = i["ssm_glu_w"][0].reshape(2, P, 4, P).transpose(1, 2, 0, 3).reshape(1, P, -1)
    o["conv_pw2"] = i["conv_pw2_w"][0].reshape(2, P, 2, P).transpose(1, 2, 0, 3).reshape(1, P, -1)
    o["w_out"] = blocks(i["w_out"][0])
    o["xa_wq"], o["xa_wk"], o["xa_wo"] = (blocks(i[n][0]) for n in ("xa_wq", "xa_wk", "xa_wo"))
    o["xa_wv"] = np.concatenate([rows(i["xa_wv"][0][:, 512 * n:512 * n + 512], 4) for n in range(2)])
    f = i["ffn_w_in"][0]
    o["ffn_in"] = f.reshape(KD, P, 2, FB, P).transpose(3, 1, 2, 0, 4).reshape(FB, P, -1)
    o["ffn_out"] = rows(i["ffn_w_out"][0], 2)
    w = i["w_in_2"][0]
    o["w2_mq"], o["w2_mk"], o["w2_mo"] = blocks(w[:, 0:512]), blocks(w[:, 512:1024]), blocks(w[:, 1536:2048])
    o["w2_gq"], o["w2_gk"], o["w2_gr"] = blocks(w[:, 2064:2320]), blocks(w[:, 2320:2576]), blocks(w[:, 3088:3600])
    o["w2_mv"], o["w2_gv"] = rows(w[:, 1024:1536], 4), rows(w[:, 2576:3088], 4)
    small = np.zeros((D, 104), np.float32)
    gates = w[:, 2048:2064].reshape(D, 2, 2, MH)
    for dr in range(2):
        for kind in range(2):
            small[:, 36 * kind + 32 * dr:36 * kind + 32 * dr + MH] = gates[:, dr, kind]
    small[:, 72:104] = w[:, 3600:3632]
    o["gates"] = small.reshape(KD, P, 104).transpose(1, 0, 2).reshape(1, P, -1)
    lr = np.zeros((32, 2, T), np.float32)
    for dr in range(2):
        lr[16 * dr:16 * dr + 16, dr] = i["gla_lr_w2_2"][0][dr]
    o["lr_w"] = lr
    o["w2_out"] = blocks(i["w_out_2"][0])
    o["peer_wq"] = blocks(i["peer_wq_2"][0])
    o["peer_keys"] = i["peer_keys_2"][0].reshape(2 * PH, NE, P).transpose(2, 0, 1).reshape(1, P, -1)
    o["peer_u"] = i["peer_u_2"][0].reshape(NE, NE, KD, P).transpose(1, 3, 2, 0).reshape(NE, P, -1)
    o["peer_v"] = i["peer_v_2"][0].reshape(NE, NE, D).transpose(1, 0, 2)
    return {n: np.ascontiguousarray(a) for n, a in o.items()}


def kernel(**inputs):
    import numpy as _np
    import concourse.bacc as _bacc
    from concourse import mybir as _mybir
    from concourse.bass_utils import run_bass_kernel_spmd as _run

    nc = _bacc.Bacc("TRN2", target_bir_lowering=False, num_devices=1)
    arrays, d = {}, {}
    for name, a in lay_out({n: _np.asarray(a) for n, a in inputs.items()}).items():
        arrays[f"in_{name}"] = a
        d[name] = nc.dram_tensor(f"in_{name}", a.shape, _mybir.dt.from_np(a.dtype), kind="ExternalInput").ap()
    d["out"] = nc.dram_tensor("out_0", (P, KD, T), _mybir.dt.float32, kind="ExternalOutput").ap()
    program(nc, d)
    r = _run(nc, [arrays], core_ids=[0])
    return _np.ascontiguousarray(r.results[0]["out_0"].transpose(1, 0, 2).reshape(D, T).T)[None]
```
